# Optimizing a Trainium2 kernel written in Bass

```python
import jax, jax.numpy as jnp
from jax import lax
import numpy as np

D_MODEL = 1024
BATCH = 1
SEQ = 512
DEPTH = 2

EPS = 1e-6
NEG_INF = -1e30
FORCE = 1e4
HEAD_DIM = 64
D_MIX = D_MODEL
GDN_HEADS = D_MIX // 4 // HEAD_DIM
GDN_WIDTH = GDN_HEADS * HEAD_DIM
GDN_CONV = 4
GDN_CHUNK = 64
NSA_HEADS = D_MIX // 2 // HEAD_DIM
NSA_WIDTH = NSA_HEADS * HEAD_DIM
NSA_KV_HEADS = 2
NSA_GROUP = NSA_HEADS // NSA_KV_HEADS
NSA_KV_WIDTH = NSA_KV_HEADS * HEAD_DIM
CMP_STRIDE = 16
CMP_LEN = 2 * CMP_STRIDE
SLC_BLOCK = 64
N_SELECT = 16
WINDOW = 512
Q_BLOCK = 128
CONV_WIDTH = D_MIX - GDN_WIDTH - NSA_WIDTH
CONV_GROUPS = 4
CONV_K = 3
ROPE_THETA = 500000.0
ROT_DIM = HEAD_DIM // 4
D_FF = ((8 * D_MODEL + 3 * 256 - 1) // (3 * 256)) * 256
IN_SIZES = (GDN_WIDTH, GDN_WIDTH, GDN_WIDTH, GDN_WIDTH, GDN_HEADS, GDN_HEADS,
            NSA_WIDTH, NSA_KV_WIDTH, NSA_KV_WIDTH, NSA_KV_WIDTH, NSA_KV_WIDTH, NSA_KV_WIDTH, NSA_KV_WIDTH,
            3 * NSA_HEADS, CONV_WIDTH, CONV_WIDTH, CONV_WIDTH)
D_IN = sum(IN_SIZES)

kernel_name = "hymba_style_gdn_nsa_shortconv_trunk"

def rms_norm(x, gain):
    xf = x.astype(jnp.float32)
    y = xf * lax.rsqrt(jnp.mean(xf * xf, axis=-1, keepdims=True) + EPS)
    return (y * gain.astype(jnp.float32)).astype(x.dtype)

def l2_norm(x):
    return x * lax.rsqrt(jnp.sum(x * x, axis=-1, keepdims=True) + EPS)

def causal_depthwise_conv(x, w):
    k = w.shape[0]
    return lax.conv_general_dilated(x, w[:, None, :].astype(x.dtype), window_strides=(1,),
                                    padding=[(k - 1, 0)], dimension_numbers=("NWC", "WIO", "NWC"),
                                    feature_group_count=x.shape[-1])

def rope_tables(positions):
    inv = jnp.float32(ROPE_THETA) ** (-jnp.arange(0, ROT_DIM, 2, dtype=jnp.float32) / ROT_DIM)
    ang = positions.astype(jnp.float32)[..., None] * inv
    return jnp.cos(ang), jnp.sin(ang)

def apply_partial_rope(x, cos, sin):
    extra = x.ndim - 3
    shp = cos.shape[:2] + (1,) * extra + cos.shape[-1:]
    c, s = cos.reshape(shp), sin.reshape(shp)
    half = ROT_DIM // 2
    x1 = x[..., :half].astype(jnp.float32)
    x2 = x[..., half:ROT_DIM].astype(jnp.float32)
    rot = jnp.concatenate([x1 * c - x2 * s, x2 * c + x1 * s], axis=-1).astype(x.dtype)
    return jnp.concatenate([rot, x[..., ROT_DIM:]], axis=-1)

def masked_softmax(scores, mask):
    s = jnp.where(mask, scores.astype(jnp.float32), NEG_INF)
    return jnp.where(mask, jax.nn.softmax(s, axis=-1), 0.0)

def gated_delta_rule(q, k, v, g, beta):
    b, T, h, dk = q.shape
    dv = v.shape[-1]
    n = T // GDN_CHUNK
    q = l2_norm(q.astype(jnp.float32)) * (dk ** -0.5)
    k = l2_norm(k.astype(jnp.float32))
    v = v.astype(jnp.float32)

    def chunks(t):
        return t.reshape(b, n, GDN_CHUNK, h, t.shape[-1]).transpose(0, 3, 1, 2, 4)

    qc, kc, vc = chunks(q), chunks(k), chunks(v)
    gc = g.astype(jnp.float32).reshape(b, n, GDN_CHUNK, h).transpose(0, 3, 1, 2)
    bc = beta.astype(jnp.float32).reshape(b, n, GDN_CHUNK, h).transpose(0, 3, 1, 2)
    gcum = jnp.cumsum(gc, axis=-1)
    tril = jnp.tril(jnp.ones((GDN_CHUNK, GDN_CHUNK), dtype=bool))
    strict = jnp.tril(jnp.ones((GDN_CHUNK, GDN_CHUNK), dtype=bool), -1)
    diff = gcum[..., :, None] - gcum[..., None, :]
    decay = jnp.where(tril, jnp.exp(jnp.where(tril, diff, 0.0)), 0.0)
    kb = kc * bc[..., None]
    a = jnp.where(strict, jnp.einsum("bhncd,bhnsd->bhncs", kb, kc) * decay, 0.0)
    ia = a + jnp.eye(GDN_CHUNK, dtype=jnp.float32)
    rhs = jnp.concatenate([vc * bc[..., None], kb * jnp.exp(gcum)[..., None]], axis=-1)
    sol = lax.linalg.triangular_solve(ia, rhs, left_side=True, lower=True, unit_diagonal=True)
    u, w = sol[..., :dv], sol[..., dv:]
    qk = jnp.where(tril, jnp.einsum("bhncd,bhnsd->bhncs", qc, kc) * decay, 0.0)
    q_dec = qc * jnp.exp(gcum)[..., None]
    k_dec = kc * jnp.exp(gcum[..., -1:] - gcum)[..., None]
    g_last = jnp.exp(gcum[..., -1])

    def step(state, xs):
        u_i, w_i, qd_i, kd_i, qk_i, gl_i = xs
        v_new = u_i - w_i @ state
        o_i = qd_i @ state + qk_i @ v_new
        state = state * gl_i[..., None, None] + jnp.einsum("bhck,bhcv->bhkv", kd_i, v_new)
        return state, o_i

    xs = tuple(jnp.moveaxis(t, 2, 0) for t in (u, w, q_dec, k_dec, qk, g_last))
    s0 = jnp.zeros((b, h, dk, dv), jnp.float32)
    _, o = lax.scan(step, s0, xs)
    return o.transpose(1, 0, 3, 2, 4).reshape(b, T, h, dv)

def compress_blocks(t, pe, w1, w2):
    b, T, g, d = t.shape
    nb = T // CMP_STRIDE
    blk = t.reshape(b, nb, CMP_STRIDE, g, d)
    win = jnp.concatenate([blk[:, :-1], blk[:, 1:]], axis=2) + pe[:, None, :].astype(t.dtype)
    flat = win.transpose(0, 1, 3, 2, 4).reshape(b, nb - 1, g, CMP_LEN * d)
    return jax.nn.gelu(flat @ w1) @ w2

def nsa_attention(q, k_cmp, v_cmp, k_slc, v_slc, k_win, v_win, gate_logits, cos, sin,
                  q_gain, k_gain, cmp_pe, cmp_w1, cmp_w2):
    b, T = q.shape[:2]
    G, R, dh = NSA_KV_HEADS, NSA_GROUP, HEAD_DIM
    kv = lambda t: t.reshape(b, T, G, dh)
    qn = rms_norm(q.reshape(b, T, G, R, dh), q_gain)
    qr = apply_partial_rope(qn, cos, sin)
    kc = rms_norm(compress_blocks(kv(k_cmp), cmp_pe[0], cmp_w1[0], cmp_w2[0]), k_gain[0])
    vc = compress_blocks(kv(v_cmp), cmp_pe[1], cmp_w1[1], cmp_w2[1])
    ks = apply_partial_rope(rms_norm(kv(k_slc), k_gain[1]), cos, sin)
    kw = apply_partial_rope(rms_norm(kv(k_win), k_gain[2]), cos, sin)
    nslc = T // SLC_BLOCK
    n_sel = min(N_SELECT, nslc)
    ks_blk = ks.reshape(b, nslc, SLC_BLOCK, G, dh).transpose(0, 3, 1, 2, 4)
    vs_blk = kv(v_slc).reshape(b, nslc, SLC_BLOCK, G, dh).transpose(0, 3, 1, 2, 4)
    pad = ((0, 0), (WINDOW, 0), (0, 0), (0, 0))
    kw_pad, vw_pad = jnp.pad(kw, pad), jnp.pad(kv(v_win), pad)
    gates = jax.nn.sigmoid(gate_logits.astype(jnp.float32)).reshape(b, T, G, R, 3)
    nc = kc.shape[1]
    cmp_end = jnp.arange(nc) * CMP_STRIDE + CMP_LEN - 1
    ratio = SLC_BLOCK // CMP_STRIDE
    frac = jnp.minimum(CMP_LEN, SLC_BLOCK - CMP_STRIDE * jnp.arange(ratio)).astype(jnp.float32) / CMP_LEN
    scale = dh ** -0.5
    b_ix = jnp.arange(b)[:, None, None, None]
    g_ix = jnp.arange(G)[None, :, None, None]

    def block(i):
        s = i * Q_BLOCK
        tq = s + jnp.arange(Q_BLOCK)
        q_n = lax.dynamic_slice_in_dim(qn, s, Q_BLOCK, 1)
        q_r = lax.dynamic_slice_in_dim(qr, s, Q_BLOCK, 1)
        gt = lax.dynamic_slice_in_dim(gates, s, Q_BLOCK, 1)
        cmask = cmp_end[None, :] <= tq[:, None]
        p_c = masked_softmax(jnp.einsum("bqgrd,bcgd->bgrqc", q_n, kc) * scale, cmask)
        o_c = jnp.einsum("bgrqc,bcgd->bqgrd", p_c.astype(vc.dtype), vc)
        imp = jnp.pad(p_c.sum(axis=2), ((0, 0), (0, 0), (0, 0), (0, 1))).reshape(b, G, Q_BLOCK, nslc, ratio)
        own, spill = imp @ frac, imp @ (1.0 - frac)
        slc = own + jnp.pad(spill[..., :-1], ((0, 0), (0, 0), (0, 0), (1, 0)))
        cur = (tq // SLC_BLOCK)[:, None]
        j = jnp.arange(nslc)[None, :]
        forced = (j == 0) | (j == cur) | (j == cur - 1)
        score = jnp.where(forced, FORCE, jnp.where(j <= cur, slc, -FORCE))
        _, idx = lax.top_k(score, n_sel)
        k_g = ks_blk[b_ix, g_ix, idx].reshape(b, G, Q_BLOCK, n_sel * SLC_BLOCK, dh)
        v_g = vs_blk[b_ix, g_ix, idx].reshape(b, G, Q_BLOCK, n_sel * SLC_BLOCK, dh)
        kpos = (idx[..., None] * SLC_BLOCK + jnp.arange(SLC_BLOCK)).reshape(b, G, Q_BLOCK, -1)
        smask = (kpos <= tq[:, None])[:, :, None]
        p_s = masked_softmax(jnp.einsum("bqgrd,bgqkd->bgrqk", q_r, k_g) * scale, smask)
        o_s = jnp.einsum("bgrqk,bgqkd->bqgrd", p_s.astype(v_g.dtype), v_g)
        kb = lax.dynamic_slice_in_dim(kw_pad, s, Q_BLOCK + WINDOW, 1)
        vb = lax.dynamic_slice_in_dim(vw_pad, s, Q_BLOCK + WINDOW, 1)
        kpos_w = s - WINDOW + jnp.arange(Q_BLOCK + WINDOW)
        dist = tq[:, None] - kpos_w[None, :]
        wmask = (dist >= 0) & (dist < WINDOW) & (kpos_w >= 0)[None, :]
        p_w = masked_softmax(jnp.einsum("bqgrd,bkgd->bgrqk", q_r, kb) * scale, wmask)
        o_w = jnp.einsum("bgrqk,bkgd->bqgrd", p_w.astype(vb.dtype), vb)
        return (gt[..., 0:1] * o_c + gt[..., 1:2] * o_s + gt[..., 2:3] * o_w).astype(q.dtype)

    out = lax.map(block, jnp.arange(T // Q_BLOCK))
    return out.transpose(1, 0, 2, 3, 4, 5).reshape(b, T, NSA_WIDTH)

def setup_inputs(seed: int = 0) -> dict:
    key = jax.random.key(seed)
    ks = jax.random.split(key, 20)
    f32 = jnp.float32
    nrm = lambda k, shp, sc: jax.random.normal(k, shp, f32) * sc
    gain = lambda k, shp: 1.0 + 0.02 * jax.random.normal(k, shp, f32)
    dt = jnp.exp(jax.random.uniform(ks[5], (DEPTH, GDN_HEADS), f32) * (jnp.log(0.1) - jnp.log(0.001)) + jnp.log(0.001))
    return {
        "x": nrm(ks[0], (BATCH, SEQ, D_MODEL), 1.0),
        "positions": jnp.tile(jnp.arange(SEQ, dtype=jnp.int32)[None, :], (BATCH, 1)),
        "attn_norm": gain(ks[1], (DEPTH, D_MODEL)),
        "w_in": nrm(ks[2], (DEPTH, D_MODEL, D_IN), D_MODEL ** -0.5),
        "gdn_conv_w": nrm(ks[3], (DEPTH, GDN_CONV, 3 * GDN_WIDTH), GDN_CONV ** -0.5),
        "gdn_a_log": jnp.log(jax.random.uniform(ks[4], (DEPTH, GDN_HEADS), f32, 1.0, 16.0)),
        "gdn_dt_bias": dt + jnp.log(-jnp.expm1(-dt)),
        "gdn_norm": gain(ks[6], (DEPTH, HEAD_DIM)),
        "nsa_q_norm": gain(ks[7], (DEPTH, HEAD_DIM)),
        "nsa_k_norm": gain(ks[8], (DEPTH, 3, HEAD_DIM)),
        "nsa_cmp_pe": nrm(ks[9], (DEPTH, 2, CMP_LEN, HEAD_DIM), 0.1),
        "nsa_cmp_w1": nrm(ks[10], (DEPTH, 2, CMP_LEN * HEAD_DIM, HEAD_DIM), (CMP_LEN * HEAD_DIM) ** -0.5),
        "nsa_cmp_w2": nrm(ks[11], (DEPTH, 2, HEAD_DIM, HEAD_DIM), HEAD_DIM ** -0.5),
        "conv_w": nrm(ks[12], (DEPTH, CONV_K, CONV_WIDTH), CONV_K ** -0.5),
        "w_out": nrm(ks[13], (DEPTH, D_MIX, D_MODEL), D_MIX ** -0.5),
        "ffn_norm": gain(ks[14], (DEPTH, D_MODEL)),
        "w_gate_up": nrm(ks[15], (DEPTH, D_MODEL, 2 * D_FF), D_MODEL ** -0.5),
        "w_down": nrm(ks[16], (DEPTH, D_FF, D_MODEL), D_FF ** -0.5),
    }

def reference(x, positions, attn_norm, w_in, gdn_conv_w, gdn_a_log, gdn_dt_bias, gdn_norm,
              nsa_q_norm, nsa_k_norm, nsa_cmp_pe, nsa_cmp_w1, nsa_cmp_w2, conv_w, w_out,
              ffn_norm, w_gate_up, w_down):
    b, T, _ = x.shape
    cos, sin = rope_tables(positions)
    split_at = [int(v) for v in np.cumsum(IN_SIZES)[:-1]]
    for l in range(DEPTH):
        h = rms_norm(x, attn_norm[l])
        proj = h @ w_in[l]
        (gq, gk, gv, gz, gb, ga, nq, kcmp, vcmp, kslc, vslc, kwin, vwin, ngate,
         cb, cc, cx) = jnp.split(proj, split_at, axis=-1)
        qkv = jax.nn.silu(causal_depthwise_conv(jnp.concatenate([gq, gk, gv], axis=-1), gdn_conv_w[l]))
        hq, hk, hv = jnp.split(qkv, 3, axis=-1)
        heads = lambda t: t.reshape(b, T, GDN_HEADS, HEAD_DIM)
        g = -jnp.exp(gdn_a_log[l].astype(jnp.float32)) * jax.nn.softplus(
            ga.astype(jnp.float32) + gdn_dt_bias[l].astype(jnp.float32))
        beta = jax.nn.sigmoid(gb.astype(jnp.float32))
        o_gdn = gated_delta_rule(heads(hq), heads(hk), heads(hv), g, beta)
        o_gdn = (rms_norm(o_gdn, gdn_norm[l]) * jax.nn.silu(heads(gz).astype(jnp.float32)))
        o_gdn = o_gdn.reshape(b, T, GDN_WIDTH).astype(x.dtype)
        o_nsa = nsa_attention(nq, kcmp, vcmp, kslc, vslc, kwin, vwin, ngate, cos, sin,
                              nsa_q_norm[l], nsa_k_norm[l], nsa_cmp_pe[l], nsa_cmp_w1[l], nsa_cmp_w2[l])
        o_conv = cb * causal_depthwise_conv(cc * cx, conv_w[l])
        mix = jnp.concatenate([o_gdn, o_nsa.astype(x.dtype), o_conv.astype(x.dtype)], axis=-1)
        x = x + mix @ w_out[l]
        h2 = rms_norm(x, ffn_norm[l])
        gate, up = jnp.split(h2 @ w_gate_up[l], 2, axis=-1)
        x = x + (jax.nn.silu(gate) * up) @ w_down[l]
    return x


_drawn_inputs = setup_inputs


def setup_inputs(seed=0):
    import zlib

    import numpy as np

    out = dict(_drawn_inputs(seed))
    spreads = {}
    factors = {'gdn_norm': 6.793, 'nsa_q_norm': 8.0, 'nsa_k_norm': 8.0, 'ffn_norm': 2.808}
    for name, (base, spread) in spreads.items():
        noise = np.random.default_rng([zlib.crc32(name.encode()), seed]).standard_normal(out[name].shape)
        drawn = base * np.exp(spread * noise) if base else spread * noise
        out[name] = __import__('jax').numpy.asarray(drawn.astype(out[name].dtype))
    for name, factor in factors.items():
        out[name] = (out[name] * factor).astype(out[name].dtype)
    return out
```

```python
from contextlib import ExitStack

import numpy as np

import concourse.bass as bass
from concourse import mybir

F32 = mybir.dt.float32
F32R = mybir.dt.float32r
BF16 = mybir.dt.bfloat16
I32 = mybir.dt.int32
ALU = mybir.AluOpType
ACT = mybir.ActivationFunctionType
AX = mybir.AxisListType.X

P = 128
EPS = 1e-6
NEG = -1e30
HEAD = 64
CMP_STRIDE, CMP_LEN = 16, 32
ROPE_THETA = 500000.0
ROT = HEAD // 4
HALF = ROT // 2
SLOT = 280
N_PARAMS = 18
OG_UNIT = 9
RSQRT_SEED = 1597463007.0


class Semaphores(dict):

    def __init__(self, nc, ctx):
        self.nc, self.ctx = nc, ctx

    def __missing__(self, name):
        self[name] = self.ctx.enter_context(self.nc.semaphore(name))
        return self[name]


class Chain:

    def __init__(self, engine, sem):
        self.engine, self.sem, self.n = engine, sem, 0

    def __call__(self, instruction):
        self.n += 1
        instruction.then_inc(self.sem, 1)
        self.engine.wait_ge(self.sem, self.n)


def trunk(nc, A, out):
    T, D = A["x"].shape[1:]
    DEPTH = A["w_in"].shape[0]
    DFF = A["w_down"].shape[1]
    NT, KD = T // P, D // P
    GH, NH, NG = D // 4 // HEAD, D // 2 // HEAD, 2
    GW, NW, KW = GH * HEAD, NH * HEAD, NG * HEAD
    NC = T // CMP_STRIDE - 1
    FT = DFF // P // 2
    assert (T, D, GH, NH) == (512, 1024, 4, 8) and FT * 2 * P == DFF

    o = np.cumsum([0, GW, GW, GW, GW, GH, GH, NW] + [KW] * 6 + [3 * NH, GW, GW, GW]).tolist()
    GQ, GK, GV, GZ, GB, GA, NQ, KC, VC, KS, VS, KWN, VWN, NGT, CB, CC, CX = o[:17]
    CHUNKS = [("cmp", KC, 256, "C"), ("gq", GQ, 256, "C"), ("gk", GK, 256, "C"), ("gv", GV, 256, "C"),
              ("zg", GZ, 264, "T"), ("kvs", KS, 256, "T"), ("kvw", KWN, 280, "T"),
              ("cc", CC, 256, "C"), ("cx", CX, 256, "C"), ("cb", CB, 256, "C"),
              ("nq0", NQ, 256, "T"), ("nq1", NQ + 256, 256, "T")]
    N_IN = len(CHUNKS)
    N_OUT = D // 256
    DOWN = [(0, 4), (4, 4), (8, FT - 8)]
    PER_HALF = FT + 2 * len(DOWN)
    FFN0 = N_IN + N_OUT
    N_CHUNKS = FFN0 + 2 * PER_HALF
    GROUPS = [(c, g, "dve" if CHUNKS[c][0] in ("cx", "cb") else "act")
              for c in range(N_IN) for g in range(2 if CHUNKS[c][3] == "C" else NT)]
    IN_BANKS = 3

    def emptied(n):
        e = GROUPS[n][2]
        return e, sum(1 for x in GROUPS[:n + 1] if x[2] == e)

    with ExitStack() as ctx:
        def sb(name, shape, dt=F32):
            return ctx.enter_context(nc.sbuf_tensor(name, shape, dt))

        ctx.enter_context(nc.allow_non_contiguous_dma(reason="small transposed parameter loads"))
        S = Semaphores(nc, ctx)
        prefetched = ctx.enter_context(nc.semaphore("prefetched"))

        x = sb("x_tok", [P, NT, D])
        hhi, hlo = sb("hT_hi", [P, KD, T], F32R), sb("hT_lo", [P, KD, T], F32R)
        raw = sb("w_raw", [P, 2, KD * SLOT])
        whi, wlo = sb("w_hi", [P, 2, KD * SLOT], F32R), sb("w_lo", [P, 2, KD * SLOT], F32R)
        ident, tri = sb("ident", [P, P]), sb("tri", [P, P])
        identb, negm = sb("identb", [P, P], BF16), sb("negm", [P, P], BF16)
        below, offblk = sb("below", [P, P], BF16), sb("offblk", [P, P], BF16)
        ones = sb("ones", [P, P])
        cneg, cok = sb("cneg", [P, NT, 32], BF16), sb("cok", [P, NT, 32], BF16)
        cossin = sb("cossin", [P, 2, NT, HALF])
        an, fn = sb("an", [P, KD]), sb("fn", [P, KD])
        cw, scw = sb("cw", [P, 6, 4]), sb("scw", [P, 2, 3])
        alog, dtb = sb("alog", [P, GH]), sb("dtb", [P, GH])
        gng, qg, kg = sb("gng", [P, HEAD]), sb("qg", [P, HEAD]), sb("kg", [P, 3, HEAD])
        pe_c = sb("pe_c", [P, 2, 16])
        w2c = sb("w2c", [HEAD, 2, HEAD])
        st = sb("st", [P, 9, 32])
        gbuf = sb("gbuf", [P, NT, 8])
        gsc = sb("gsc", [P, 9, NT * GH])
        ngt = sb("ngt", [P, NT, 3 * NH])
        peb = sb("peb", [HEAD, 2])
        vcr = sb("vcr", [P, HEAD])
        kcT = sb("kcT", [P, 2, 32])
        state = sb("state", [P, 2, P])
        glc = sb("glc", [P, NT, 2])
        att = sb("att", [P, 2, 4, NT])
        ffn = ExitStack()
        ahi = ffn.enter_context(nc.sbuf_tensor("aT_hi", [P, FT, T], F32R))
        alo = ffn.enter_context(nc.sbuf_tensor("aT_lo", [P, FT, T], F32R))
        ft = ffn.enter_context(nc.sbuf_tensor("ffn_tmp", [P, 4, T], F32))
        ffn.close()
        arena = sb("arena", [P, 24584])
        ps = ctx.enter_context(nc.psum_tensor("ps", [P, 8, 512], F32))

        def at(off, *shape):
            v = arena[:, off:off + int(np.prod(shape))]
            if len(shape) == 2:
                return v.rearrange("p (a b) -> p a b", a=shape[0])
            if len(shape) == 3:
                return v.rearrange("p (a b c) -> p a b c", a=shape[0], b=shape[1])
            if len(shape) == 4:
                return v.rearrange("p (a b c d) -> p a b c d", a=shape[0], b=shape[1], c=shape[2])
            return v

        hn = at(15360, NT, D)
        junk = at(19456, D)
        gtm = at(0, NT, 3 * GW)
        cM, cMT, cM2, cM2T, cM4T, cZ1 = (at(512 * i, GH, P) for i in range(6))
        qT, kT, qdT = (at(3072 + 1024 * i, 2, T) for i in range(3))
        L = at(6144, NT * GH, P)
        x2 = at(6144, 2, 2, T)
        qd = at(6144, NT, GW)
        vb, kdec = at(8192, NT, GW), at(9216, NT, GW)
        dA, dB = at(10240, GH, P), at(10752, GH, P)
        wT = at(10240, 2, T)
        TD, TDT = at(11264, NT * GH, P), at(13312, NT * GH, P)
        w1c = at(11264, 2, 16, HEAD)
        hid = at(10240, 3, 2 * 2 * NC)[0:HEAD]
        kcn = at(10240 + 12 * NC, 2, P)[0:32]
        gpre = at(15360, 2, 516)
        gcm = at(15360 + 1032, 2, T)
        ccb = at(15360, 2, T)
        cpre = at(15360 + 1024, 2, 514)
        kbe = at(17416, NT, GW)
        og = at(17416, NT, GW)
        qkT = at(18440, NT * GH, P)
        Dm, Ti = at(20488, 16, 16), at(20488 + 256, 16, 16)
        Tt, dtmp = at(20488 + 512, 16, 16), at(20488 + 768, 16, 16)
        trig = at(13312, 2, GH * P)
        nq = at(3072, NT, NW)
        z = at(21512, NT, GW)
        kv = at(22536, NT, 4 * KW)
        qnT = at(0, 4, T)
        qhl = at(2048, NH, P)
        khl = at(20488, 4, P)
        Pc, PcT = at(20488, 2, 16, 32), at(4096, 2, T)
        vnew = at(3072, GW)
        jq = at(16384, 2, NW)
        rot = at(16384, 3, NT * NH * HALF)
        zt = at(16384, NT, GW)
        prob = [at(11264 + 1280 * i, 1280) for i in range(2)]
        pT = [at(13824 + 512 * i, T) for i in range(3)]
        qst = hhi
        kst = hlo
        MIX_LO = [0, 5, 1, 2, 3, 4, 6, 7]
        d_in = nc.dram_tensor("diag_in", [8, 16, 16, 16], F32).ap()
        d_out = nc.dram_tensor("diag_out", [2, 8, 16, 16, 16], F32).ap()

        def slot(buf, c, kt, w):
            return buf[:, c % 2, 0:kt * w].rearrange("p (k n) -> p k n", k=kt)

        def chunk_shape(c):
            if c < N_IN:
                return KD, CHUNKS[c][2]
            if c < FFN0:
                return KD, 256
            i = (c - FFN0) % PER_HALF
            return (KD, 256) if i < FT else (DOWN[(i - FT) % 3][1], 512)

        with nc.Block() as block:
            @block.sync
            def _(sp):
                sp.dma_start(x[:], A["x"][0].rearrange("(t p) d -> p t d", p=P)).then_inc(S["x_in"], 16)
                sp.dma_start(st[:, 0, 0:NT].bitcast(I32), A["positions"].rearrange("o (t p) -> p (o t)", p=P)
                             ).then_inc(S["pos_in"], 16)
                for c in range(2):
                    _, c0, w, _ = CHUNKS[c]
                    sp.dma_start(slot(raw, c, KD, w), A["w_in"][0].rearrange("(k p) n -> p k n", p=P)[:, :, c0:c0 + w]
                                 ).then_inc(prefetched, 16)
                sp.wait_ge(S["x_in"], 16)

            @block.gpsimd
            def _(pool):
                chain = Chain(pool, S["pool_chain"])

                def select(t, base, pattern, cm, op, fill):
                    chain(nc.gpsimd.affine_select(out=t, in_=t, compare_op=op, fill=fill, base=base,
                                                  pattern=pattern, channel_multiplier=cm))

                for t, v in ((ident, 0.0), (identb, 0.0), (tri, 1.0), (below, 1.0), (offblk, 1.0), (negm, 0.0),
                             (ones, 1.0), (cneg, 0.0), (cok, 1.0), (state, 0.0)):
                    chain(nc.gpsimd.memset(t[:], v))
                for t in (ident, identb):
                    select(t[:], 0, [[-1, P]], 1, ALU.not_equal, 1.0)
                select(tri[:], 0, [[1, P]], -1, ALU.is_ge, 0.0)
                select(below[:], -1, [[-1, P]], 1, ALU.is_ge, 0.0)
                select(negm[:], 0, [[-1, P]], 1, ALU.is_ge, NEG)
                select(offblk[:].rearrange("p (b j) -> p b j", b=8), -16, [[-16, 8], [0, 16]], 1, ALU.is_ge, 0.0)
                for m, fill in ((cneg, NEG), (cok, 0.0)):
                    select(m[:], -(CMP_LEN - 1), [[P, NT], [-CMP_STRIDE, 32]], 1, ALU.is_ge, fill)

            @block.vector
            def _(dve):
                chain = Chain(dve, S["dve_chain"])
                dve.wait_ge(S["pos_in"], 16)
                chain(nc.vector.tensor_copy(st[:, 1, 0:NT], st[:, 0, 0:NT].bitcast(I32)))
                ang, k, r = (st[:, 2 + i, 0:NT * HALF].rearrange("p (t f) -> p t f", t=NT) for i in range(3))
                for f in range(HALF):
                    inv = float(np.float32(np.float64(np.float32(ROPE_THETA)) ** (-2.0 * f / ROT)))
                    chain(nc.vector.tensor_scalar(ang[:, :, f], st[:, 1, 0:NT], inv, None, ALU.mult))
                two_pi = 2 * np.pi
                c1 = 6.28125
                c2 = float(np.float32(np.floor((two_pi - c1) * 2 ** 20) / 2 ** 20))
                c3 = float(np.float32(two_pi - c1 - c2))
                magic = 12582912.0
                for i, shift in ((0, np.pi / 2), (1, 0.0)):
                    chain(nc.vector.tensor_scalar(k, ang, float(1 / two_pi), float(shift / two_pi), ALU.mult, ALU.add))
                    chain(nc.vector.tensor_scalar(k, k, magic, None, ALU.add))
                    chain(nc.vector.tensor_scalar(k, k, magic, None, ALU.subtract))
                    chain(nc.vector.tensor_copy(r, ang))
                    for cst in (c1, c2, c3):
                        chain(nc.vector.scalar_tensor_tensor(out=r, in0=k, scalar=-cst, in1=r, op0=ALU.mult, op1=ALU.add))
                    chain(nc.vector.tensor_scalar(r, r, float(shift), 3.1415925, ALU.add, ALU.min))
                    chain(nc.vector.tensor_scalar(cossin[:, i], r, -3.1415925, None, ALU.max))
                dve.nop().then_inc(S["angles"], 1)

            @block.scalar
            def _(act):
                act.wait_ge(S["angles"], 1)
                nc.scalar.activation(cossin[:], cossin[:], ACT.Sin).then_inc(S["rope"], 1)
                act.wait_ge(S["rope"], 1)

        def clear():
            nc.all_engine_barrier()
            ids = sorted(s.num for s in S.values())
            assert ids == list(range(ids[0], ids[-1] + 1))
            nc.gpsimd.sem_clear(range(ids[0], ids[-1] + 1))
            nc.all_engine_barrier()

        clear()

        def mm_count(c):
            n = 0
            for i in range(c + 1):
                if i < N_IN:
                    n += 2 if CHUNKS[i][3] == "C" else NT
                elif i < FFN0:
                    n += NT
                else:
                    n += 2 if (i - FFN0) % PER_HALF < FT else NT
            return n

        def loads(c):
            return sum(2 if i >= FFN0 and (i - FFN0) % PER_HALF < FT else 1 for i in range(2 + c % 2, c + 1, 2))

        HOP_GROUP = 24
        SLC, WIN = 0, 1

        with nc.Fori(0, DEPTH) as l:
            with nc.Block() as block:
                @block.sync
                def _(sp):
                    for dst, src in ((an[:], A["attn_norm"][l].rearrange("(k p) -> p k", p=P)),
                                     (fn[:], A["ffn_norm"][l].rearrange("(k p) -> p k", p=P))):
                        sp.dma_start(dst, src).then_inc(S["norm_gains"], 16)

                    def row(name, n):
                        return A[name][l].rearrange("(o n) -> o n", o=1).broadcast_to([P, n])

                    params = [
                        (w1c[:, 0], A["nsa_cmp_w1"][l, 0].rearrange("(m p) j -> p m j", p=P)),
                        (w1c[:, 1], A["nsa_cmp_w1"][l, 1].rearrange("(m p) j -> p m j", p=P)),
                        (w2c[:], A["nsa_cmp_w2"][l].rearrange("k i d -> i k d")),
                        (scw[:, 0], A["conv_w"][l].rearrange("k (j p) -> j p k", p=P)[0]),
                        (scw[:, 1], A["conv_w"][l].rearrange("k (j p) -> j p k", p=P)[1]),
                        (alog[:], row("gdn_a_log", GH)), (dtb[:], row("gdn_dt_bias", GH)),
                        (gng[:], row("gdn_norm", HEAD)), (qg[:], row("nsa_q_norm", HEAD)),
                        (kg[:].rearrange("p a d -> p (a d)"),
                         A["nsa_k_norm"][l].rearrange("(o a) d -> o (a d)", o=1).broadcast_to([P, 3 * HEAD])),
                    ]
                    params += [(cw[:, j], A["gdn_conv_w"][l].rearrange("k (j p) -> j p k", p=P)[j]) for j in range(6)]
                    params += [(pe_c[:, k], A["nsa_cmp_pe"][l, k].rearrange("(m r) d -> (r d) m", r=2)) for k in range(2)]
                    assert len(params) == N_PARAMS
                    for dst, src in params:
                        sp.dma_start(dst, src).then_inc(S["params"], 16)

                    for c in range(2, N_CHUNKS):
                        sp.wait_ge(S["w_lo"], c - 1)
                        kt, w = chunk_shape(c)
                        if c < N_IN:
                            src = A["w_in"][l].rearrange("(k p) n -> p k n", p=P)[:, :, CHUNKS[c][1]:CHUNKS[c][1] + w]
                            dst = slot(raw, c, kt, w)
                        elif c < FFN0:
                            n0 = (c - N_IN) * 256
                            src = A["w_out"][l].rearrange("(k p) n -> p k n", p=P)[:, :, n0:n0 + 256]
                            dst = slot(raw, c, kt, w)
                        else:
                            f, i = divmod(c - FFN0, PER_HALF)
                            if i < FT:
                                n0 = (f * FT + i) * P
                                src = A["w_gate_up"][l].rearrange("(k p) n -> p k n", p=P)
                                sp.dma_start(slot(raw, c, kt, w)[:, :, 0:P], src[:, :, n0:n0 + P]).then_inc(S[f"w_in{c % 2}"], 16)
                                src = src[:, :, DFF + n0:DFF + n0 + P]
                                dst = slot(raw, c, kt, w)[:, :, P:2 * P]
                            else:
                                ch, (k0, _) = (i - FT) // 3, DOWN[(i - FT) % 3]
                                r0 = (f * FT + k0) * P
                                src = A["w_down"][l][r0:r0 + kt * P].rearrange("(k p) n -> p k n", p=P)[:, :, ch * 512:ch * 512 + 512]
                                dst = slot(raw, c, kt, w)
                        sp.dma_start(dst, src).then_inc(S[f"w_in{c % 2}"], 16)
                    for c in range(2):
                        sp.wait_ge(S["w_lo"], N_CHUNKS - 1 + c)
                        _, c0, w, _ = CHUNKS[c]
                        sp.dma_start(slot(raw, c, KD, w),
                                     A["w_in"][(l + 1) % DEPTH].rearrange("(k p) n -> p k n", p=P)[:, :, c0:c0 + w]
                                     ).then_inc(prefetched, 16)

                @block.tensor
                def _(pe):
                    def norm_transposes(tag):
                        pe.wait_ge(S["hn" + tag], 1)
                        for k in range(KD):
                            if k >= 4:
                                pe.wait_ge(S["hlo" + tag], k - 3)
                            for t in range(NT):
                                mm = nc.tensor.transpose(ps[:, k % 4, t * P:(t + 1) * P], hn[:, t, k * P:(k + 1) * P], ident[:])
                            mm.then_inc(S["hps" + tag], 1)

                    def three_pass(out_ap, a, b, part, kts, first, last, sem=None):
                        ab, bb = ((0, 0), (0, 1), (1, 0))[part]
                        for i, k in enumerate(kts):
                            mm = nc.tensor.matmul(out_ap, a(ab, k), b(bb, k), start=first and i == 0,
                                                  stop=last and i == len(kts) - 1)
                        if sem is not None:
                            mm.then_inc(sem, 1)

                    def in_group(n, part):
                        c, g, _ = GROUPS[n]
                        _, _, w, kind = CHUNKS[c]
                        if part == 0:
                            if g == 0:
                                pe.wait_ge(S["w_lo"], c + 1)
                            if n >= IN_BANKS:
                                e, v = emptied(n - IN_BANKS)
                                pe.wait_ge(S["ev_" + e], v)
                            else:
                                pe.wait_ge(S["hlo0"], KD)
                        W = (slot(whi, c, KD, w), slot(wlo, c, KD, w))
                        h = (hhi, hlo)
                        bank = n % IN_BANKS
                        done = S["mm"] if part == 2 else None
                        if kind == "C":
                            three_pass(ps[:, bank, :], lambda b, k: W[b][:, k, g * P:(g + 1) * P], lambda b, k: h[b][:, k, :],
                                       part, range(KD), part == 0, part == 2, done)
                        else:
                            three_pass(ps[:, bank, 0:w], lambda b, k: h[b][:, k, g * P:(g + 1) * P], lambda b, k: W[b][:, k, :],
                                       part, range(KD), part == 0, part == 2, done)

                    def cmp_first():
                        pe.wait_ge(S["ev_act"], 2)
                        pe.wait_ge(S["params"], 16 * N_PARAMS)
                        for k in range(2):
                            for m in range(16):
                                nc.tensor.matmul(ps[0:HEAD, 3, k * P:k * P + 2 * NC].rearrange("p (g n) -> p g n", g=2),
                                                 w1c[:, k, m, :], x2[:, k, :, 2 * m:2 * m + CMP_STRIDE * (NC - 1) + 1:CMP_STRIDE],
                                                 start=(k == 0 and m == 0), stop=(m == 15), skip_group_check=True)
                            for m in range(16):
                                mm = nc.tensor.matmul(ps[0:HEAD, 3, k * P + 2 * NC:k * P + 2 * NC + 1], w1c[:, k, m, :],
                                                      pe_c[:, k, m:m + 1], start=False, stop=(m == 15), skip_group_check=True)
                        mm.then_inc(S["cmp"], 1)

                    def cmp_second():
                        pe.wait_ge(S["cmp_hid"], 1)
                        for k in range(2):
                            for g in range(NG):
                                mm = nc.tensor.matmul(ps[0:NC, 7, (k * 2 + g) * HEAD:(k * 2 + g + 1) * HEAD],
                                                      hid[:, 0, k * 2 * NC + g * NC:k * 2 * NC + (g + 1) * NC], w2c[:, k, :],
                                                      start=True, stop=True)
                        mm.then_inc(S["cmp"], 1)

                    def cmp_third():
                        pe.wait_ge(S["cmp_kn"], 1)
                        nc.tensor.transpose(ps[:, 7, 0:NC], kcn[0:NC, 0, :], ident[0:NC, 0:NC]).then_inc(S["cmp"], 1)

                    def gdn_transpose(j):
                        pe.wait_ge(S["conv"], j + 1)
                        if j >= 3:
                            pe.wait_ge(S["gtm"], j - 2)
                        if j == 0:
                            pe.wait_ge(S["cmp_hid"], 1)
                        for t in range(NT):
                            mm = nc.tensor.transpose(ps[:, 3 + j % 3, t * P:(t + 1) * P], gcm[:, j % 2, t * P:(t + 1) * P], ident[:])
                        mm.then_inc(S["gtr"], 1)

                    def gdn_back(i, bank):
                        pe.wait_ge(S["qdec"] if i >= 4 else S["qkn"], 1)
                        if i == 0:
                            pe.wait_ge(S["gtm"], 6)
                        if i == 4:
                            pe.wait_ge(S["scan"], 1)
                        if i == 5:
                            pe.wait_ge(S["gT"], 1)
                        for t in range(NT):
                            src = qd[:, t, (i % 2) * P:(i % 2 + 1) * P] if i >= 4 else gtm[:, t, i * P:(i + 1) * P]
                            mm = nc.tensor.transpose(ps[:, bank, t * P:(t + 1) * P], src, ident[:])
                        mm.then_inc(S["gback"], 1)

                    def gdn_cumsum():
                        pe.wait_ge(S["g"], 1)
                        pe.wait_ge(S["kcT"], 1)
                        nc.tensor.matmul(ps[:, 7, 0:16], tri[:], gsc[:, 0, :], start=True, stop=True)
                        nc.tensor.matmul(ps[:, 7, 16:32], ones[:], gsc[:, 0, :], start=False, stop=True,
                                         skip_group_check=True).then_inc(S["gsum"], 1)

                    def gdn_grams(t):
                        pe.wait_ge(S["trig"], t + 1)
                        pe.wait_ge(S["gT"], 6)
                        if t >= 1:
                            pe.wait_ge(S["dec"], t)
                            pe.wait_ge(S["A"], t)
                        nc.tensor.matmul(ps[:, 7, :], ones[:], trig[:, t % 2, :], start=True, stop=True).then_inc(S["gr"], 1)
                        cols = slice(t * P, (t + 1) * P)
                        for par in range(2):
                            rows = slice(par * HEAD, (par + 1) * HEAD)
                            for j in range(2):
                                nc.tensor.matmul(ps[:, 3 + par, j * P:(j + 1) * P], kT[rows, j, cols], kT[rows, j, cols],
                                                 start=(j == 0), stop=True, skip_group_check=True)
                        for par in range(2):
                            rows = slice(par * HEAD, (par + 1) * HEAD)
                            for j in range(2):
                                mm = nc.tensor.matmul(ps[:, 5 + par, j * P:(j + 1) * P], kT[rows, j, cols], qT[rows, j, cols],
                                                      start=(j == 0), stop=True, skip_group_check=True)
                        mm.then_inc(S["gram"], 1)

                    def batch(bank, lhs, rhs):
                        for h in range(GH):
                            mm = nc.tensor.matmul(ps[:, bank, h * P:(h + 1) * P], lhs(h), rhs(h), start=True, stop=True)
                        return mm

                    def hop(s):
                        t, i = divmod(s, 7)
                        q = t * GH
                        if i == 0:
                            if t == 0:
                                pe.wait_ge(S["Lmask"], 1)
                                pe.wait_ge(S["TD"], 256)
                                pe.wait_ge(S["A"], 4)
                            else:
                                pe.wait_ge(S["hop_dve"], 6 * t)
                                pe.wait_ge(S["hop_act"], 4 * t)
                            batch(4, lambda h: L[:, q + h, :], lambda h: TDT[:, q + h, :])
                            mm = batch(5, lambda h: TDT[:, q + h, :], lambda h: L[:, q + h, :])
                        elif i == 1:
                            pe.wait_ge(S["hop_dve"], 6 * t + 1)
                            pe.wait_ge(S["hop_act"], 4 * t + 1)
                            batch(6, lambda h: cMT[:, h, :], lambda h: cM[:, h, :])
                            mm = batch(7, lambda h: cM[:, h, :], lambda h: cMT[:, h, :])
                        elif i == 2:
                            pe.wait_ge(S["hop_dve"], 6 * t + 2)
                            pe.wait_ge(S["hop_act"], 4 * t + 2)
                            mm = batch(4, lambda h: cM2[:, h, :], lambda h: cM2T[:, h, :])
                        elif i == 3:
                            pe.wait_ge(S["hop_dve"], 6 * t + 3)
                            mm = batch(5, lambda h: cM4T[:, h, :], lambda h: TD[:, q + h, :])
                        elif i == 4:
                            pe.wait_ge(S["hop_dve"], 6 * t + 4)
                            mm = batch(6, lambda h: cM2T[:, h, :], lambda h: cZ1[:, h, :])
                        elif i == 5:
                            pe.wait_ge(S["hop_dve"], 6 * t + 5)
                            pe.wait_ge(S["hop_pool"], t + 1)
                            mm = batch(7, lambda h: cM[:, h, :], lambda h: cMT[:, h, :])
                        else:
                            pe.wait_ge(S["hop_act"], 4 * t + 3)
                            for h in range(GH):
                                nc.tensor.matmul(ps[:, 3, h * HEAD:(h + 1) * HEAD], cM4T[:, h, :], vb[:, t, h * HEAD:(h + 1) * HEAD],
                                                 start=True, stop=True)
                            for h in range(GH):
                                par, j = h % 2, h // 2
                                mm = nc.tensor.matmul(ps[par * HEAD:(par + 1) * HEAD, 4, j * P:(j + 1) * P],
                                                      kbe[:, t, h * HEAD:(h + 1) * HEAD], cM4T[:, h, :],
                                                      start=True, stop=True)
                        mm.then_inc(S["hop"], 1)

                    norm_transposes("0")
                    slots = 0
                    for n in range(len(GROUPS)):
                        for part in range(3):
                            in_group(n, part)
                            if n >= HOP_GROUP and slots < 7 * NT:
                                hop(slots)
                                slots += 1
                        if n == 3:
                            cmp_first()
                        if 4 <= n <= 9:
                            gdn_transpose(n - 4)
                        if n == 5:
                            cmp_second()
                        if n == 7:
                            cmp_third()
                        if n == 11:
                            for i in range(4):
                                gdn_back(i, 3 + i)
                        if n == 12:
                            gdn_cumsum()
                        if n == 14:
                            gdn_back(4, 7)
                            gdn_back(5, 3)
                        if 15 <= n <= 18:
                            gdn_grams(n - 15)
                    assert slots == 7 * NT

                    pe.wait_ge(S["qn"], 1)
                    pe.wait_ge(S["hop_act"], 4 * NT)
                    pe.wait_ge(S["hop_dve"], 6 * NT)
                    e, v = emptied(len(GROUPS) - 1)
                    pe.wait_ge(S["ev_" + e], v)
                    for j in range(4):
                        for t in range(NT):
                            mm = nc.tensor.transpose(ps[:, j, t * P:(t + 1) * P], nq[:, t, j * P:(j + 1) * P], ident[:])
                        mm.then_inc(S["qnps"], 1)
                    for t in range(NT):
                        pe.wait_ge(S["qkhl"], t + 1)
                        if t >= 1:
                            pe.wait_ge(S["qstv"], t)
                            pe.wait_ge(S["qsta"], t)
                        for h in range(NH):
                            mm = nc.tensor.transpose(ps[:, 4 + h // 4, (h % 4) * P:(h % 4 + 1) * P], qhl[:, h, :], ident[:])
                        for i in range(4):
                            mm = nc.tensor.transpose(ps[:, 6, i * P:(i + 1) * P], khl[:, i, :], ident[:])
                        mm.then_inc(S["qkps"], 1)
                    pe.wait_ge(S["qnT"], 4)
                    pe.wait_ge(S["kcT"], 1)
                    for par in range(2):
                        for j in range(4):
                            for t in range(NT):
                                mm = nc.tensor.matmul(ps[:, par, (j * 4 + t) * 32:(j * 4 + t) * 32 + NC],
                                                      qnT[par * HEAD:(par + 1) * HEAD, j, t * P:(t + 1) * P],
                                                      kcT[par * HEAD:(par + 1) * HEAD, j // 2, 0:NC],
                                                      start=(j == 0 and t == 0), stop=True, skip_group_check=True)
                    mm.then_inc(S["csc"], 1)
                    pe.wait_ge(S["cprob"], 1)
                    for par in range(2):
                        for t in range(NT):
                            mm = nc.tensor.transpose(ps[:, 2 + par, t * P:(t + 1) * P],
                                                     Pc[:, par, 4 * t:4 * t + 4, :].rearrange("p j c -> p (j c)"), ident[:])
                    mm.then_inc(S["cpt"], 1)

                    def scores(u):
                        h, br = divmod(u, 2)
                        g = h // 4
                        for i in range(NT):
                            if u >= 1:
                                pe.wait_ge(S["exp"], 4 * (u - 1) + i + 1)
                            elif i == 0:
                                pe.wait_ge(S["PcT"], 2)
                                pe.wait_ge(S["qstv"], NT)
                                pe.wait_ge(S["qsta"], NT)
                            n = max(256, (i + 1) * P)
                            q_ap = qst[:, h, i * P:(i + 1) * P]
                            nc.tensor.matmul(ps[:, i, 0:n], q_ap, kst[:, br * 2 + g, 0:n], start=True, stop=False)
                            nc.tensor.matmul(ps[:, i, 0:n], q_ap, kst[:, 4 + br * 2 + g, 0:n], start=False, stop=True)
                            nc.tensor.matmul(ps[:, i, i * P:(i + 1) * P], identb[:], negm[:], start=False, stop=True,
                                             skip_group_check=True).then_inc(S["score"], 1)

                    def p_transpose(u, j):
                        k = 4 * u + j
                        if j == 0:
                            pe.wait_ge(S["pscaled"], u + 1)
                        if k >= 2:
                            pe.wait_ge(S["pTe"], k - 1)
                        for i in range(j, NT):
                            o0 = i * (i + 1) // 2 * P + j * P
                            mm = nc.tensor.transpose(ps[:, 4 + k % 2, (i - j) * P:(i - j + 1) * P], prob[u % 2][:, o0:o0 + P], ident[:])
                        mm.then_inc(S["ptr"], 1)

                    def pv(u, j):
                        h, br = divmod(u, 2)
                        k = 4 * u + j
                        pe.wait_ge(S["pTe"], k + 1)
                        v0 = br * 256 + P + (h // 4) * HEAD
                        nc.tensor.matmul(ps[(h % 2) * HEAD:(h % 2 + 1) * HEAD, 6, j * P:T], kv[:, j, v0:v0 + HEAD],
                                         pT[k % 3][:, 0:(NT - j) * P], start=False, stop=br == 1,
                                         skip_group_check=True).then_inc(S["pv"], 1)

                    def cmp_pv(h):
                        par, j = h % 2, h // 2
                        if h == 0:
                            pe.wait_ge(S["PcT"], 2)
                        if par == 0 and h >= 2:
                            pe.wait_ge(S["mix_lo"], h // 2)
                        nc.tensor.matmul(ps[par * HEAD:(par + 1) * HEAD, 6, :], vcr[32 * j:32 * j + NC, :],
                                         PcT[32 * j:32 * j + NC, par, :], start=True, stop=False, skip_group_check=True)

                    def recur_first(t):
                        if t >= 1:
                            pe.wait_ge(S["state"], t)
                        for j in range(2):
                            mm = nc.tensor.matmul(ps[:, 7, j * P:(j + 1) * P], wT[:, j, t * P:(t + 1) * P], state[:, j, :],
                                                  start=(j == 0), stop=True, skip_group_check=True)
                        mm.then_inc(S["wS"], 1)

                    def recur_second(t):
                        pe.wait_ge(S["vnew"], t + 1)
                        for j in range(2):
                            nc.tensor.matmul(ps[:, 7, j * P:(j + 1) * P], kdec[:, t, j * P:(j + 1) * P], vnew[:, j * P:(j + 1) * P],
                                             start=(j == 0), stop=True, skip_group_check=True)
                        for j in range(2):
                            nc.tensor.matmul(ps[:, 7, 256 + j * P:256 + (j + 1) * P], qdT[:, j, t * P:(t + 1) * P], state[:, j, :],
                                             start=False, stop=False, skip_group_check=True)
                        for h in range(GH):
                            c0 = 256 + h * HEAD
                            mm = nc.tensor.matmul(ps[:, 7, c0:c0 + HEAD], qkT[:, t * GH + h, :], vnew[:, h * HEAD:(h + 1) * HEAD],
                                                  start=False, stop=True, skip_group_check=True)
                        mm.then_inc(S["oS"], 1)

                    def gdn_out(m):
                        pe.wait_ge(S["og"], 1)
                        if m == 1:
                            pe.wait_ge(S["mixg_lo"], 1)
                        for t in range(NT):
                            mm = nc.tensor.transpose(ps[:, 7, t * P:(t + 1) * P], og[:, t, m * P:(m + 1) * P], ident[:])
                        mm.then_inc(S["ogT"], 1)

                    scores(0)
                    for u in range(2 * NH):
                        if u + 1 < 2 * NH:
                            scores(u + 1)
                        if u < 2 * NT:
                            (recur_second if u % 2 else recur_first)(u // 2)
                        if u == OG_UNIT:
                            gdn_out(0)
                        if u == OG_UNIT + 1:
                            gdn_out(1)
                        p_transpose(u, 0)
                        if u % 2 == 0:
                            cmp_pv(u // 2)
                        p_transpose(u, 1)
                        pv(u, 0)
                        p_transpose(u, 2)
                        pv(u, 1)
                        p_transpose(u, 3)
                        pv(u, 2)
                        pv(u, 3)

                    pe.wait_ge(S["mixg_lo"], 2)
                    pe.wait_ge(S["mixc_lo"], 2)
                    for c in range(N_IN, FFN0):
                        pe.wait_ge(S["w_lo"], c + 1)
                        W = (slot(whi, c, KD, 256), slot(wlo, c, KD, 256))
                        mix = (lambda k: ahi[:, k, :], lambda k: alo[:, MIX_LO[k], :])
                        for t in range(NT):
                            if c > N_IN:
                                pe.wait_ge(S["x_res"], 4 * (c - N_IN - 1) + t + 1)
                            if c == N_IN and t == 0:
                                ready = [0, 1, 6, 7, 2, 3, 4]
                                for part in range(3):
                                    three_pass(ps[:, 0, 0:256], lambda b, k: mix[b](k)[:, 0:P], lambda b, k: W[b][:, k, :],
                                               part, ready, part == 0, False)
                                pe.wait_ge(S["mix_lo"], 4)
                                for part in range(3):
                                    three_pass(ps[:, 0, 0:256], lambda b, k: mix[b](k)[:, 0:P], lambda b, k: W[b][:, k, :],
                                               part, [5], False, part == 2, S["mm"] if part == 2 else None)
                                continue
                            for part in range(3):
                                three_pass(ps[:, t, 0:256], lambda b, k: mix[b](k)[:, t * P:(t + 1) * P], lambda b, k: W[b][:, k, :],
                                           part, range(KD), part == 0, part == 2, S["mm"] if part == 2 else None)

                    norm_transposes("1")
                    for f in range(2):
                        for i in range(FT):
                            c, cnt = FFN0 + f * PER_HALF + i, f * FT + i
                            pe.wait_ge(S["w_lo"], c + 1)
                            W = (slot(whi, c, KD, 256), slot(wlo, c, KD, 256))
                            h = (hhi, hlo)
                            if cnt == 0:
                                pe.wait_ge(S["hlo1"], KD)
                            for s in range(2):
                                if i >= 2:
                                    pe.wait_ge(S["up_mul"] if s else S["silu"], cnt - 1)
                                elif f == 1:
                                    pe.wait_ge(S["x_down"], 4 + 2 * i + s + 1)
                                for part in range(3):
                                    three_pass(ps[:, 2 * (i % 2) + s, :], lambda b, k: W[b][:, k, s * P:(s + 1) * P],
                                               lambda b, k: h[b][:, k, :], part, range(KD), part == 0, part == 2,
                                               S["mm"] if part == 2 else None)
                        for ch in range(2):
                            for q, (k0, kn) in enumerate(DOWN):
                                c = FFN0 + f * PER_HALF + FT + ch * 3 + q
                                pe.wait_ge(S["w_lo"], c + 1)
                                if ch == 0:
                                    pe.wait_ge(S["a_lo"], f * FT + k0 + kn)
                                W = (slot(whi, c, kn, 512), slot(wlo, c, kn, 512))
                                a = (ahi, alo)
                                for t in range(NT):
                                    if q == 0 and f == 1 and ch == 0:
                                        pe.wait_ge(S["x_down"], t + 1)
                                    for part in range(3):
                                        three_pass(ps[:, (4 if ch == 0 else 0) + t, :],
                                                   lambda b, k: a[b][:, k0 + k, t * P:(t + 1) * P], lambda b, k: W[b][:, k, :],
                                                   part, range(kn), q == 0 and part == 0, q == 2 and part == 2,
                                                   S["mm"] if part == 2 else None)

                @block.scalar
                def _(act):
                    chain = Chain(act, S["act_chain"])

                    def split_hi(c):
                        if c >= N_CHUNKS:
                            return
                        if c < 2:
                            act.wait_ge(prefetched, 32 * (l + 1))
                        else:
                            act.wait_ge(S[f"w_in{c % 2}"], 16 * loads(c))
                            act.wait_ge(S["mm"], mm_count(c - 2))
                        kt, w = chunk_shape(c)
                        nc.scalar.activation(whi[:, c % 2, 0:kt * w], raw[:, c % 2, 0:kt * w], ACT.Copy).then_inc(S["w_hi"], 1)

                    def norm_squares(tag):
                        for t in range(NT):
                            if tag == "1":
                                act.wait_ge(S["x_res"], 12 + t + 1)
                            chain(nc.scalar.activation(junk, x[:, t, :], ACT.Square, accum_out=st[:, 0, t:t + 1]))
                        act.nop().then_inc(S["ssq" + tag], 1)

                    def norm_hi(tag, gain):
                        for k in range(KD):
                            act.wait_ge(S["hps" + tag], k + 1)
                            nc.scalar.activation(hhi[:, k, :], ps[:, k % 4, :], ACT.Copy, scale=gain[:, k:k + 1]
                                                 ).then_inc(S["hhi" + tag], 1)

                    def ev(dst, src):
                        return nc.scalar.activation(dst, src, ACT.Copy)

                    def empty_group(n):
                        c, g, _ = GROUPS[n]
                        name = CHUNKS[c][0]
                        act.wait_ge(S["mm"], n + 1)
                        b = ps[:, n % IN_BANKS, :]
                        if name == "cmp":
                            for gg in range(2):
                                rows = slice(gg * HEAD, (gg + 1) * HEAD)
                                ev(x2[0:HEAD, g, gg, :], b[rows, :])
                                i = ev(x2[HEAD:P, g, gg, 0:T - 1], b[rows, 1:T])
                        elif name in ("gq", "gk", "gv"):
                            j = n - 2
                            if j >= 2:
                                act.wait_ge(S["conv"], j - 1)
                            i = ev(gpre[:, j % 2, 0:T], b[:, :])
                        elif name == "zg":
                            ev(z[:, g, :], b[:, 0:GW])
                            i = ev(gbuf[:, g, :], b[:, GW:GW + 2 * GH])
                        elif name == "kvs":
                            i = ev(kv[:, g, 0:256], b[:, 0:256])
                        elif name == "kvw":
                            ev(kv[:, g, 256:512], b[:, 0:256])
                            i = ev(ngt[:, g, :], b[:, 256:256 + 3 * NH])
                        elif name == "cc":
                            act.wait_ge(S["conv"], 6)
                            i = ev(ccb[:, g, :], b[:, :])
                        else:
                            if name == "nq0" and g == 0:
                                act.wait_ge(S["gram"], NT)
                            q0 = 0 if name == "nq0" else 256
                            i = ev(nq[:, g, q0:q0 + 256], b[:, 0:256])
                        i.then_inc(S["ev_act"], 1)

                    def hop_act(s):
                        t, i = divmod(s, 7)
                        if i not in (0, 1, 5, 6):
                            return
                        act.wait_ge(S["hop"], s + 1)
                        dst, bank = {0: (cM, 5), 1: (cM2, 6), 5: (cM4T, 7), 6: (vb[:, t, :], 3)}[i]
                        if i == 6:
                            ev(dst, ps[:, bank, 0:GW]).then_inc(S["hop_act"], 1)
                        else:
                            ev(dst, ps[:, bank, :].rearrange("p (h c) -> p h c", h=GH)).then_inc(S["hop_act"], 1)

                    norm_squares("0")
                    split_hi(0)
                    split_hi(1)
                    act.wait_ge(S["norm_gains"], 32)
                    norm_hi("0", an)
                    slots = 0
                    for n in range(len(GROUPS)):
                        c, g, e = GROUPS[n]
                        last = n + 1 == len(GROUPS) or GROUPS[n + 1][0] != c
                        if n >= HOP_GROUP:
                            for _ in range(2):
                                if slots < 7 * NT:
                                    hop_act(slots)
                                    slots += 1
                        if last:
                            split_hi(c + 2)
                        if e == "act":
                            empty_group(n)
                        if n >= HOP_GROUP and slots < 7 * NT:
                            hop_act(slots)
                            slots += 1
                        if n == 4:
                            act.wait_ge(S["cmp_u"], 1)
                            nc.scalar.activation(hid[:, 2, :], hid[:, 1, :], ACT.Tanh, scale=0.7978845608028654
                                                 ).then_inc(S["cmp_th"], 1)
                        if 2 <= n <= 7:
                            j = n - 2
                            act.wait_ge(S["cy"], j + 1)
                            nc.scalar.activation(gpre[:, j % 2, 0:T], gcm[:, j % 2, :], ACT.Tanh).then_inc(S["th"], 1)
                        if 4 <= n <= 9:
                            j = n - 4
                            act.wait_ge(S["gtr"], j + 1)
                            ev(gtm[:, :, j * P:(j + 1) * P], ps[:, 3 + j % 3, :].rearrange("p (t c) -> p t c", t=NT)
                               ).then_inc(S["gtm"], 1)
                        if n == 8:
                            act.wait_ge(S["gtm"], 4)
                            nc.scalar.activation(L.rearrange("p (t a) b -> p t (a b)", t=NT), gtm[:, :, 0:2 * GW],
                                                 ACT.Square).then_inc(S["gsq"], 1)
                        if n == 11:
                            act.wait_ge(S["gy"], 1)
                            nc.scalar.activation(gsc[:, 1, :].rearrange("p (t h) -> p t h", t=NT), gbuf[:, :, 0:GH],
                                                 ACT.Tanh, scale=0.5)
                            nc.scalar.activation(alog[:], alog[:], ACT.Exp)
                            nc.scalar.activation(gsc[:, 8, :], gsc[:, 8, :], ACT.Exp, scale=-1.0).then_inc(S["gexp"], 1)
                            act.wait_ge(S["gexp1"], 1)
                            nc.scalar.activation(gsc[:, 8, :], gsc[:, 8, :], ACT.Ln).then_inc(S["gln"], 1)
                            for i in range(4):
                                act.wait_ge(S["gback"], i + 1)
                                ev((qT, qT, kT, kT)[i][:, i % 2, :], ps[:, 3 + i, :]).then_inc(S["gT"], 1)
                        if n == 12:
                            act.wait_ge(S["gcum"], 1)
                            nc.scalar.activation(gsc[:, 3, :], gsc[:, 2, :], ACT.Exp)
                            nc.scalar.activation(gsc[:, 5, :], gsc[:, 5, :], ACT.Exp)
                            nc.scalar.activation(gsc[:, 6, :], gsc[:, 7, :], ACT.Exp).then_inc(S["geg"], 1)
                        if n == 14:
                            for i in range(2):
                                act.wait_ge(S["gback"], 5 + i)
                                ev(qdT[:, i, :], ps[:, 7 if i == 0 else 3, :]).then_inc(S["gT"], 1)
                        if 15 <= n <= 18:
                            t = n - 15
                            act.wait_ge(S["dec"], t + 1)
                            nc.scalar.activation(dA, dA, ACT.Exp, scale=-1.0)
                            nc.scalar.activation(dB, dB, ACT.Exp).then_inc(S["dexp"], 1)
                        if n == 18:
                            act.wait_ge(S["A"], NT)
                            for b in range(8):
                                act.dma_start(d_in[b].rearrange("q i j -> i q j"), L[16 * b:16 * b + 16, :, 16 * b:16 * b + 16]
                                              ).then_inc(S["d_in"], 16)
                            act.wait_ge(S["d_in"], 128)
                            act.dma_start(Dm.rearrange("p i j -> p (i j)"), d_in.rearrange("b q i j -> (b q) (i j)")
                                          ).then_inc(S["Dm"], 16)
                        if n == 21:
                            act.wait_ge(S["Tt"], 1)
                            for s, src in enumerate((Ti, Tt)):
                                act.dma_start(d_out[s].rearrange("b q i j -> (b q) (i j)"), src.rearrange("p i j -> p (i j)")
                                              ).then_inc(S["d_out"], 16)
                            act.wait_ge(S["d_out"], 32)
                            act.wait_ge(S["tdzero"], 1)
                            for s, dst in enumerate((TD, TDT)):
                                for b in range(8):
                                    act.dma_start(dst[16 * b:16 * b + 16, :, 16 * b:16 * b + 16],
                                                  d_out[s, b].rearrange("q i j -> i q j")).then_inc(S["TD"], 16)

                    nc.scalar.activation(ngt[:], ngt[:], ACT.Tanh, scale=0.5).then_inc(S["ngth"], 1)
                    act.wait_ge(S["cbdone"], 1)
                    for i in range(2 * NT):
                        t, which = i // 2, i % 2
                        if i >= 2:
                            act.wait_ge(S["qred"], i - 1)
                        elif i == 0:
                            act.wait_ge(S["ev_act"], emptied(len(GROUPS) - 1)[1])
                        nc.scalar.activation(jq[:, which, :], (kv if which else nq)[:, t, :], ACT.Square).then_inc(S["qsq"], 1)
                    for j in range(4):
                        act.wait_ge(S["qnps"], j + 1)
                        ev(qnT[:, j, :], ps[:, j, :]).then_inc(S["qnT"], 1)
                    for t in range(NT):
                        act.wait_ge(S["roped"], 1)
                        if t >= 1:
                            act.wait_ge(S["qkps"], t)
                        nc.scalar.activation(qhl[:, :, 0:HEAD].bitcast(F32R), nq[:, t, :].rearrange("p (h d) -> p h d", h=NH), ACT.Copy)
                        for br in range(2):
                            ins = nc.scalar.activation(khl[:, 2 * br:2 * br + 2, 0:HEAD].bitcast(F32R),
                                                       kv[:, t, br * 256:br * 256 + P].rearrange("p (g d) -> p g d", g=2), ACT.Copy)
                        ins.then_inc(S["qkhi"], 1)
                        act.wait_ge(S["qkps"], t + 1)
                        cols = slice(t * P, (t + 1) * P)
                        ev(qst[:, 0:4, cols], ps[:, 4, :].rearrange("p (h c) -> p h c", h=4))
                        for r in range(2):
                            ins = ev(kst[r * HEAD:(r + 1) * HEAD, 0:4, cols], ps[0:HEAD, 6, :].rearrange("p (h c) -> p h c", h=4))
                        ins.then_inc(S["qsta"], 1)
                    act.wait_ge(S["cmax"], 1)
                    nc.scalar.activation(Pc, Pc, ACT.Exp, scale=0.125).then_inc(S["cexp"], 1)
                    act.wait_ge(S["cpt"], 1)
                    for par in range(2):
                        ev(PcT[:, par, :], ps[:, 2 + par, :]).then_inc(S["PcT"], 1)

                    def exps(u):
                        act.wait_ge(S["nmax"], u + 1)
                        if u >= 2:
                            act.wait_ge(S["ptr"], 4 * (u - 2) + 4)
                        for i in range(NT):
                            o0, n = i * (i + 1) // 2 * P, (i + 1) * P
                            nc.scalar.activation(prob[u % 2][:, o0:o0 + n], ps[:, i, 0:n], ACT.Exp, bias=att[:, 0, u % 2, i:i + 1],
                                                 scale=0.125, accum_out=att[:, 1, u % 2, i:i + 1]).then_inc(S["exp"], 1)

                    def mix_hi(m):
                        act.wait_ge(S["pv"], 16 * (m + 1))
                        ev(ahi[:, 2 + m, :], ps[:, 6, :]).then_inc(S["mix_hi"], 1)

                    exps(0)
                    for u in range(2 * NH):
                        for j in range(NT):
                            k = 4 * u + j
                            act.wait_ge(S["ptr"], k + 1)
                            if k >= 3:
                                act.wait_ge(S["pv"], k - 2)
                            ev(pT[k % 3][:, 0:(NT - j) * P], ps[:, 4 + k % 2, 0:(NT - j) * P]).then_inc(S["pTe"], 1)
                        if u == OG_UNIT - 1:
                            act.wait_ge(S["oall"], 1)
                            nc.scalar.activation(zt, og, ACT.Square).then_inc(S["osq"], 1)
                            act.wait_ge(S["ored"], 1)
                            nc.scalar.activation(zt, z, ACT.Tanh, scale=0.5).then_inc(S["zth"], 1)
                            for m in range(2):
                                ev(ahi[:, 6 + m, :], ccb[:, m, :]).then_inc(S["mixc_hi"], 1)
                        if u in (OG_UNIT, OG_UNIT + 1):
                            m = u - OG_UNIT
                            act.wait_ge(S["ogT"], m + 1)
                            ev(ahi[:, m, :], ps[:, 7, :]).then_inc(S["mixg_hi"], 1)
                        if u + 1 < 2 * NH:
                            exps(u + 1)
                        if u % 4 == 3:
                            mix_hi(u // 4)

                    for c in range(N_IN, FFN0):
                        split_hi(c + 2)
                    norm_squares("1")
                    norm_hi("1", fn)
                    for f in range(2):
                        for i in range(FT):
                            c, cnt = FFN0 + f * PER_HALF + i, f * FT + i
                            split_hi(c + 2)
                            act.wait_ge(S["mm"], mm_count(c) - 1)
                            if cnt >= 2:
                                act.wait_ge(S["up_mul"], cnt - 1)
                            nc.scalar.activation(ft[:, cnt % 2, :], ps[:, 2 * (i % 2), :], ACT.Silu).then_inc(S["silu"], 1)
                            act.wait_ge(S["up_mul"], cnt + 1)
                            ev(ahi[:, i, :], ft[:, 2 + cnt % 2, :]).then_inc(S["a_hi"], 1)
                        for i in range(FT, PER_HALF):
                            split_hi(FFN0 + f * PER_HALF + i + 2)

                @block.gpsimd
                def _(pool):
                    chain = Chain(pool, S["pool_chain"])

                    def split_lo(c):
                        if c >= N_CHUNKS:
                            return
                        pool.wait_ge(S["w_hi"], c + 1)
                        kt, w = chunk_shape(c)
                        nc.gpsimd.tensor_tensor(wlo[:, c % 2, 0:kt * w], raw[:, c % 2, 0:kt * w],
                                                whi[:, c % 2, 0:kt * w].bitcast(F32), ALU.subtract).then_inc(S["w_lo"], 1)

                    def scaled(dst, src, row):
                        s = gsc[:, row, :].rearrange("p (t h o) -> p t h o", t=NT, o=1).broadcast_to([P, NT, GH, HEAD])
                        return nc.gpsimd.tensor_tensor(dst.rearrange("p t (h d) -> p t h d", h=GH),
                                                       src.rearrange("p t (h d) -> p t h d", h=GH), s, ALU.mult)

                    def make_trig(t):
                        if t >= 2:
                            pool.wait_ge(S["gr"], t - 1)
                        for h in range(GH):
                            ins = nc.gpsimd.tensor_scalar(trig[:, t % 2, h * P:(h + 1) * P], tri[:],
                                                          gsc[:, 0, t * GH + h:t * GH + h + 1], None, ALU.mult)
                        ins.then_inc(S["trig"], 1)

                    def one_minus(t):
                        pool.wait_ge(S["hop"], 7 * t + 2)
                        pool.wait_ge(S["hop_dve"], 6 * t + 1)
                        idb = ident[:].rearrange("p (o c) -> p o c", o=1).broadcast_to([P, GH, P])
                        nc.gpsimd.tensor_tensor(cMT, idb, cMT, ALU.subtract).then_inc(S["hop_pool"], 1)

                    nc.gpsimd.memset(state[:], 0.0).then_inc(S["szero"], 1)
                    split_lo(0)
                    split_lo(1)
                    pool.wait_ge(S["hps0"], KD)
                    chain(nc.gpsimd.memset(Ti, 0.0))
                    nc.gpsimd.affine_select(out=Ti, in_=Ti, compare_op=ALU.not_equal, fill=1.0, base=0,
                                            pattern=[[-1, 16], [1, 16]], channel_multiplier=0).then_inc(S["tiinit"], 1)
                    split_lo(2)
                    split_lo(3)
                    split_lo(4)
                    split_lo(5)
                    split_lo(6)
                    pool.wait_ge(S["g"], 1)
                    make_trig(0)
                    make_trig(1)
                    pool.wait_ge(S["geg2"], 1)
                    pool.wait_ge(S["gtm"], 6)
                    pool.wait_ge(S["qkn"], 1)
                    scaled(qd, gtm[:, :, 0:GW], 3).then_inc(S["qdec"], 1)
                    scaled(kbe, gtm[:, :, GW:2 * GW], 4)
                    scaled(kdec, gtm[:, :, GW:2 * GW], 5)
                    scaled(vb, gtm[:, :, 2 * GW:3 * GW], 1).then_inc(S["vbs"], 1)
                    split_lo(7)
                    make_trig(2)
                    make_trig(3)
                    split_lo(8)
                    pool.wait_ge(S["cmp"], 1)
                    pool.wait_ge(S["gr"], NT)
                    nc.gpsimd.memset(at(11264, 4096), 0.0).then_inc(S["tdzero"], 1)
                    pool.wait_ge(S["d_in"], 128)
                    ob = offblk[:].rearrange("p (o c) -> p o c", o=1).broadcast_to([P, NT * GH, P])
                    nc.gpsimd.tensor_tensor(L, L, ob, ALU.mult).then_inc(S["Lmask"], 1)
                    split_lo(9)
                    split_lo(10)
                    one_minus(0)
                    split_lo(11)
                    one_minus(1)
                    one_minus(2)
                    split_lo(12)
                    one_minus(3)
                    for c in range(13, N_CHUNKS):
                        split_lo(c)

                @block.vector
                def _(dve):
                    chain = Chain(dve, S["dve_chain"])
                    V = nc.vector

                    def rsqrt(y, v, t):
                        chain(V.tensor_scalar(y.bitcast(I32), v.bitcast(I32), -0.5, RSQRT_SEED, ALU.mult, ALU.add))
                        for _ in range(3):
                            chain(V.tensor_tensor(t, y, y, ALU.mult))
                            chain(V.scalar_tensor_tensor(out=t, in0=t, scalar=-0.5, in1=v, op0=ALU.mult, op1=ALU.mult))
                            chain(V.scalar_tensor_tensor(out=y, in0=t, scalar=1.5, in1=y, op0=ALU.add, op1=ALU.mult))

                    def norm(tag, gain):
                        dve.wait_ge(S["ssq" + tag], 1)
                        chain(V.tensor_scalar(st[:, 1, 0:NT], st[:, 0, 0:NT], 1.0 / D, EPS, ALU.mult, ALU.add))
                        rsqrt(st[:, 2, 0:NT], st[:, 1, 0:NT], st[:, 3, 0:NT])
                        for t in range(NT):
                            ins = V.tensor_scalar(hn[:, t, :], x[:, t, :], st[:, 2, t:t + 1], None, ALU.mult)
                        ins.then_inc(S["hn" + tag], 1)
                        for k in range(KD):
                            dve.wait_ge(S["hhi" + tag], k + 1)
                            V.scalar_tensor_tensor(out=hlo[:, k, :], in0=ps[:, k % 4, :], scalar=gain[:, k:k + 1],
                                                   in1=hhi[:, k, :].bitcast(F32), op0=ALU.mult, op1=ALU.subtract
                                                   ).then_inc(S["hlo" + tag], 1)

                    def conv(j):
                        dve.wait_ge(S["ev_act"], j + 3)
                        if j >= 2:
                            dve.wait_ge(S["gtr"], j - 1)
                        y, v = gcm[:, j % 2, :], gpre[:, j % 2, :]
                        chain(V.tensor_scalar(y, v[:, 0:T], cw[:, j, 3:4], None, ALU.mult))
                        for d in range(1, 4):
                            ins = V.scalar_tensor_tensor(out=y[:, d:T], in0=v[:, 0:T - d], scalar=cw[:, j, 3 - d:4 - d],
                                                         in1=y[:, d:T], op0=ALU.mult, op1=ALU.add)
                            if d < 3:
                                chain(ins)
                        ins.then_inc(S["cy"], 1)
                        dve.wait_ge(S["th"], j + 1)
                        V.scalar_tensor_tensor(out=y, in0=v[:, 0:T], scalar=1.0, in1=y, op0=ALU.add, op1=ALU.mult
                                               ).then_inc(S["conv"], 1)

                    def cmp_hidden():
                        dve.wait_ge(S["cmp"], 1)
                        for k in range(2):
                            chain(V.tensor_copy(peb[:, k:k + 1], ps[0:HEAD, 3, k * P + 2 * NC:k * P + 2 * NC + 1]))
                        for k in range(2):
                            cols = slice(k * 2 * NC, (k + 1) * 2 * NC)
                            chain(V.tensor_scalar(hid[:, 0, cols], ps[0:HEAD, 3, k * P:k * P + 2 * NC], peb[:, k:k + 1], None, ALU.add))
                        chain(V.tensor_tensor(hid[:, 1, :], hid[:, 0, :], hid[:, 0, :], ALU.mult))
                        chain(V.tensor_scalar(hid[:, 1, :], hid[:, 1, :], 0.044715, 1.0, ALU.mult, ALU.add))
                        V.tensor_tensor(hid[:, 1, :], hid[:, 1, :], hid[:, 0, :], ALU.mult).then_inc(S["cmp_u"], 1)
                        dve.wait_ge(S["cmp_th"], 1)
                        chain(V.scalar_tensor_tensor(out=hid[:, 1, :], in0=hid[:, 2, :], scalar=1.0, in1=hid[:, 0, :],
                                                     op0=ALU.add, op1=ALU.mult))
                        V.tensor_scalar(hid[:, 0, :], hid[:, 1, :], 0.5, None, ALU.mult).then_inc(S["cmp_hid"], 1)

                    def cmp_norm():
                        dve.wait_ge(S["cmp"], 2)
                        chain(V.tensor_copy(kcn[0:NC, 0, :], ps[0:NC, 7, 0:P]))
                        for j in range(4):
                            chain(V.tensor_copy(vcr[32 * j:32 * j + NC, :], ps[0:NC, 7, P + (j // 2) * HEAD:P + (j // 2 + 1) * HEAD]))
                        chain(V.tensor_tensor(kcn[0:NC, 1, :], kcn[0:NC, 0, :], kcn[0:NC, 0, :], ALU.mult))
                        chain(V.tensor_reduce(st[0:NC, 4, 0:2], kcn[0:NC, 1, :].rearrange("p (g d) -> p g d", g=2), AX, ALU.add))
                        chain(V.tensor_scalar(st[0:NC, 5, 0:2], st[0:NC, 4, 0:2], 1.0 / HEAD, EPS, ALU.mult, ALU.add))
                        rsqrt(st[0:NC, 6, 0:2], st[0:NC, 5, 0:2], st[0:NC, 7, 0:2])
                        for g in range(NG):
                            ins = V.scalar_tensor_tensor(out=kcn[0:NC, 0, g * HEAD:(g + 1) * HEAD], in0=kcn[0:NC, 0, g * HEAD:(g + 1) * HEAD],
                                                         scalar=st[0:NC, 6, g:g + 1], in1=kg[0:NC, 0, :], op0=ALU.mult, op1=ALU.mult)
                        ins.then_inc(S["cmp_kn"], 1)

                    def cmp_keys():
                        dve.wait_ge(S["cmp"], 3)
                        for g in range(NG):
                            for r in range(2):
                                ins = V.tensor_copy(kcT[r * HEAD:(r + 1) * HEAD, g, 0:NC], ps[g * HEAD:(g + 1) * HEAD, 7, 0:NC])
                        ins.then_inc(S["kcT"], 1)

                    def per_head(r, n, rows=None):
                        return r.rearrange("p (n o) -> p n o", o=1).broadcast_to([P, n, HEAD])

                    def l2_norms():
                        dve.wait_ge(S["gsq"], 1)
                        chain(V.tensor_reduce(st[:, 0, :], L.rearrange("p a (b d) -> p (a b) d", d=HEAD), AX, ALU.add))
                        chain(V.tensor_scalar(st[:, 1, :], st[:, 0, :], EPS, None, ALU.add))
                        rsqrt(st[:, 2, :], st[:, 1, :], st[:, 3, :])
                        q_r = st[:, 2, :].rearrange("p (t a) -> p t a", t=NT)[:, :, 0:GH]
                        chain(V.tensor_scalar(q_r, q_r, HEAD ** -0.5, None, ALU.mult))
                        r4 = st[:, 2, :].rearrange("p (t a o) -> p t a o", t=NT, o=1).broadcast_to([P, NT, 2 * GH, HEAD])
                        v = gtm[:, :, 0:2 * GW].rearrange("p t (a d) -> p t a d", d=HEAD)
                        V.tensor_tensor(v, v, r4, ALU.mult).then_inc(S["qkn"], 1)

                    def gates():
                        y, a = gsc[:, 7, :], gsc[:, 8, :]
                        th4 = lambda r: r.rearrange("p (t h) -> p t h", t=NT)
                        row4 = lambda v: v[:].rearrange("p (o h) -> p o h", o=1).broadcast_to([P, NT, GH])
                        dve.wait_ge(S["ev_act"], 12)
                        chain(V.tensor_tensor(th4(y), gbuf[:, :, GH:2 * GH], row4(dtb), ALU.add))
                        V.scalar_tensor_tensor(out=a, in0=y, scalar=-1.0, in1=y, op0=ALU.mult, op1=ALU.max).then_inc(S["gy"], 1)
                        dve.wait_ge(S["gexp"], 1)
                        chain(V.tensor_scalar(gsc[:, 1, :], gsc[:, 1, :], 0.5, 0.5, ALU.mult, ALU.add))
                        V.tensor_scalar(a, a, 1.0, None, ALU.add).then_inc(S["gexp1"], 1)
                        dve.wait_ge(S["gln"], 1)
                        chain(V.scalar_tensor_tensor(out=a, in0=y, scalar=0.0, in1=a, op0=ALU.max, op1=ALU.add))
                        V.scalar_tensor_tensor(out=th4(gsc[:, 0, :]), in0=th4(a), scalar=-1.0, in1=row4(alog), op0=ALU.mult,
                                               op1=ALU.mult).then_inc(S["g"], 1)

                    def gate_sums():
                        dve.wait_ge(S["gsum"], 1)
                        chain(V.tensor_copy(gsc[:, 2, :], ps[:, 7, 0:16]))
                        chain(V.tensor_copy(gsc[:, 7, :], ps[:, 7, 16:32]))
                        V.tensor_tensor(gsc[:, 5, :], gsc[:, 7, :], gsc[:, 2, :], ALU.subtract).then_inc(S["gcum"], 1)
                        dve.wait_ge(S["geg"], 1)
                        V.tensor_tensor(gsc[:, 4, :], gsc[:, 1, :], gsc[:, 3, :], ALU.mult).then_inc(S["geg2"], 1)
                        for par in range(2):
                            rows = slice(par * HEAD, (par + 1) * HEAD)
                            ins = V.tensor_copy(glc[rows], gsc[rows, 6, :].rearrange("p (t j r) -> p t j r", t=NT, r=2)[:, :, :, par])
                        ins.then_inc(S["scan"], 1)

                    def decays(t):
                        dve.wait_ge(S["gr"], t + 1)
                        for h in range(GH):
                            g0 = gsc[:, 2, t * GH + h:t * GH + h + 1]
                            V.tensor_scalar(dA[:, h, :], ps[:, 7, h * P:(h + 1) * P], g0, 0.0, ALU.subtract, ALU.max)
                            ins = V.tensor_scalar(dB[:, h, :], ps[:, 7, h * P:(h + 1) * P], g0, 0.0, ALU.subtract, ALU.min)
                        ins.then_inc(S["dec"], 1)
                        dve.wait_ge(S["dexp"], t + 1)
                        for h in range(GH):
                            ins = V.scalar_tensor_tensor(out=dA[:, h, :], in0=dA[:, h, :], scalar=gsc[:, 1, t * GH + h:t * GH + h + 1],
                                                         in1=below[:], op0=ALU.mult, op1=ALU.mult)
                        chain(V.tensor_tensor(dB, dB, tri[:].rearrange("p (o c) -> p o c", o=1).broadcast_to([P, GH, P]), ALU.mult))
                        dve.wait_ge(S["gram"], t + 1)
                        for par in range(2):
                            q0 = t * GH + par
                            for bank, dec, dst in ((3 + par, dA, L), (5 + par, dB, qkT)):
                                ins = V.tensor_tensor(dst[:, q0:q0 + 3:2, :], ps[:, bank, 0:256].rearrange("p (j c) -> p j c", j=2),
                                                      dec[:, par:par + 3:2, :], ALU.mult)
                        ins.then_inc(S["A"], 1)

                    def diag_solve():
                        dve.wait_ge(S["Dm"], 16)
                        dve.wait_ge(S["tiinit"], 1)
                        for i in range(1, 16):
                            a = Ti[:, 0:i, 0:i].rearrange("p j m -> p m j")
                            d = Dm[:, i:i + 1, 0:i].broadcast_to([P, i, i])
                            tmp = dtmp[:, 0:i, 0:i]
                            chain(V.tensor_tensor(tmp, a, d, ALU.mult))
                            chain(V.tensor_reduce(Ti[:, i, 0:i], tmp, AX, ALU.add, negate=True))
                        V.tensor_copy(Tt, Ti.rearrange("p i j -> p j i")).then_inc(S["Tt"], 1)

                    def short_conv(m):
                        v, y = cpre[:, m, 0:T], ccb[:, m, :]
                        chain(V.tensor_scalar(y, v, scw[:, m, 2:3], None, ALU.mult))
                        for d in range(1, 3):
                            chain(V.scalar_tensor_tensor(out=y[:, d:T], in0=v[:, 0:T - d], scalar=scw[:, m, 2 - d:3 - d],
                                                         in1=y[:, d:T], op0=ALU.mult, op1=ALU.add))

                    def hop_dve(s):
                        t, i = divmod(s, 7)
                        if i == 5:
                            return
                        dve.wait_ge(S["hop"], s + 1)
                        if i == 2 or i == 3:
                            pass
                        bank = {0: 4, 1: 7, 2: 4, 3: 5, 4: 6, 6: 4}[i]
                        src = ps[:, bank, :].rearrange("p (h c) -> p h c", h=GH)
                        if i == 0:
                            ins = V.tensor_copy(cMT, src)
                        elif i == 1:
                            ins = V.tensor_copy(cM2T, src)
                        elif i == 2:
                            ins = V.tensor_copy(cM4T, src)
                        elif i == 3:
                            ins = V.tensor_tensor(cZ1, src, TD[:, t * GH:(t + 1) * GH, :], ALU.add)
                        elif i == 4:
                            ins = V.tensor_tensor(cM, src, cZ1, ALU.add)
                        else:
                            ins = V.tensor_copy(wT[:, :, t * P:(t + 1) * P], ps[:, 4, 0:256].rearrange("p (j c) -> p j c", j=2))
                        ins.then_inc(S["hop_dve"], 1)

                    dve.wait_ge(S["norm_gains"], 32)
                    norm("0", an)
                    dve.wait_ge(S["params"], 16 * N_PARAMS)
                    chain(V.tensor_scalar(cw[:], cw[:], 0.5, None, ALU.mult))
                    slots = 0
                    for n in range(len(GROUPS)):
                        name, g = CHUNKS[GROUPS[n][0]][0], GROUPS[n][1]
                        if n >= HOP_GROUP:
                            for _ in range(2):
                                if slots < 7 * NT:
                                    hop_dve(slots)
                                    slots += 1
                        if n == 4:
                            cmp_hidden()
                        if name in ("gq", "gk", "gv"):
                            conv(n - 2)
                        if n == 5:
                            cmp_norm()
                        if n == 7:
                            cmp_keys()
                        if n == 8:
                            l2_norms()
                        if n == 11:
                            gates()
                        if n == 12:
                            gate_sums()
                        if 15 <= n <= 18:
                            decays(n - 15)
                        if n == 19:
                            diag_solve()
                        if name == "cx":
                            dve.wait_ge(S["mm"], n + 1)
                            dve.wait_ge(S["ev_act"], 22)
                            dve.wait_ge(S["gtr"], 6)
                            V.tensor_tensor(cpre[:, g, 0:T], ps[:, n % IN_BANKS, :], ccb[:, g, :], ALU.mult).then_inc(S["ev_dve"], 1)
                            dve.wait_ge(S["ev_dve"], g + 1)
                            short_conv(g)
                        if name == "cb":
                            dve.wait_ge(S["mm"], n + 1)
                            V.tensor_tensor(ccb[:, g, :], ps[:, n % IN_BANKS, :], ccb[:, g, :], ALU.mult).then_inc(S["ev_dve"], 1)
                        if n == 25:
                            dve.wait_ge(S["ev_dve"], 4)
                            dve.nop().then_inc(S["cbdone"], 1)
                        if n >= HOP_GROUP and slots < 7 * NT:
                            hop_dve(slots)
                            slots += 1

                    dve.wait_ge(S["ngth"], 1)
                    chain(V.tensor_scalar(ngt[:], ngt[:], 0.5, 0.5, ALU.mult, ALU.add))
                    ss = st[:, 0:2, :].rearrange("p a b -> p (a b)")
                    for i in range(2 * NT):
                        dve.wait_ge(S["qsq"], i + 1)
                        V.tensor_reduce(ss[:, i * 8:(i + 1) * 8], jq[:, i % 2, :].rearrange("p (a d) -> p a d", d=HEAD), AX, ALU.add
                                        ).then_inc(S["qred"], 1)
                    dve.wait_ge(S["qred"], 2 * NT)
                    vv, rr, tt = (st[:, 2 + 2 * i:4 + 2 * i, :].rearrange("p a b -> p (a b)") for i in range(3))
                    chain(V.tensor_scalar(vv, ss, 1.0 / HEAD, EPS, ALU.mult, ALU.add))
                    rsqrt(rr, vv, tt)
                    r3 = rr.rearrange("p (t w a o) -> p t w a o", t=NT, w=2, o=1)
                    q4 = nq.rearrange("p t (h d) -> p t h d", h=NH)
                    chain(V.tensor_tensor(q4, q4, r3[:, :, 0].broadcast_to([P, NT, NH, HEAD]), ALU.mult))
                    V.tensor_tensor(nq.rearrange("p t (h d) -> p (t h) d", h=NH), nq.rearrange("p t (h d) -> p (t h) d", h=NH),
                                    qg[:].rearrange("p (o d) -> p o d", o=1).broadcast_to([P, NT * NH, HEAD]), ALU.mult
                                    ).then_inc(S["qn"], 1)
                    k4 = []
                    for br in range(2):
                        k = kv[:, :, br * 256:br * 256 + P].rearrange("p t (g d) -> p t g d", g=NG)
                        k4.append(k)
                        chain(V.tensor_tensor(k, k, r3[:, :, 1, 4 * br:4 * br + 2].broadcast_to([P, NT, NG, HEAD]), ALU.mult))
                        chain(V.tensor_tensor(k, k, kg[:, 1 + br:2 + br, :].rearrange("p (o a) d -> p o a d", o=1)
                                              .broadcast_to([P, NT, NG, HEAD]), ALU.mult))
                    dve.wait_ge(S["qnps"], 4)
                    for v, n in ((q4, NH), (k4[0], NG), (k4[1], NG)):
                        cs, sn = (cossin[:, i].rearrange("p t (o f) -> p t o f", o=1).broadcast_to([P, NT, n, HALF]) for i in range(2))
                        x1c, x2s, x1s = (rot[:, i, 0:NT * n * HALF].rearrange("p (t h f) -> p t h f", t=NT, f=HALF) for i in range(3))
                        lo_, hi_ = v[:, :, :, 0:HALF], v[:, :, :, HALF:ROT]
                        chain(V.tensor_tensor(x1c, lo_, cs, ALU.mult))
                        chain(V.tensor_tensor(x2s, hi_, sn, ALU.mult))
                        chain(V.tensor_tensor(x1s, lo_, sn, ALU.mult))
                        chain(V.tensor_tensor(lo_, x1c, x2s, ALU.subtract))
                        chain(V.tensor_tensor(x1c, hi_, cs, ALU.mult))
                        chain(V.tensor_tensor(hi_, x1c, x1s, ALU.add))
                    dve.nop().then_inc(S["roped"], 1)
                    for t in range(NT):
                        dve.wait_ge(S["qkhi"], t + 1)
                        V.tensor_tensor(qhl[:, :, HEAD:P], nq[:, t, :].rearrange("p (h d) -> p h d", h=NH), qhl[:, :, 0:HEAD], ALU.subtract)
                        for br in range(2):
                            ins = V.tensor_tensor(khl[:, 2 * br:2 * br + 2, HEAD:P], k4[br][:, t], khl[:, 2 * br:2 * br + 2, 0:HEAD],
                                                  ALU.subtract)
                        ins.then_inc(S["qkhl"], 1)
                        dve.wait_ge(S["qkps"], t + 1)
                        cols = slice(t * P, (t + 1) * P)
                        V.tensor_copy(qst[:, 4:8, cols], ps[:, 5, :].rearrange("p (h c) -> p h c", h=4))
                        for r in range(2):
                            ins = V.tensor_copy(kst[r * HEAD:(r + 1) * HEAD, 4:8, cols], ps[HEAD:P, 6, :].rearrange("p (h c) -> p h c", h=4))
                        ins.then_inc(S["qstv"], 1)

                    dve.wait_ge(S["csc"], 1)
                    chain(V.memset(Pc, 2 * NEG))
                    for par in range(2):
                        chain(V.tensor_tensor(Pc[:, par].rearrange("p (t j) c -> p j t c", j=4)[:, :, :, 0:NC],
                                              ps[:, par, :].rearrange("p (j t c) -> p j t c", j=4, t=NT)[:, :, :, 0:NC],
                                              cneg[:, :, 0:NC].rearrange("p (o t) c -> p o t c", o=1).broadcast_to([P, 4, NT, NC]), ALU.add))
                    pc = Pc.rearrange("p a b c -> p (a b) c")
                    cst, cfac = st[:, 0, :], st[:, 1, :]
                    chain(V.tensor_reduce(cst, pc[:, :, 0:NC], AX, ALU.max))
                    bc = lambda r: r.rearrange("p (n o) -> p n o", o=1).broadcast_to([P, 32, 32])
                    V.tensor_tensor(pc, pc, bc(cst), ALU.subtract).then_inc(S["cmax"], 1)
                    dve.wait_ge(S["cexp"], 1)
                    chain(V.tensor_reduce(cst, pc[:, :, 0:NC], AX, ALU.add))
                    chain(V.reciprocal(cst, cst))
                    for par in range(2):
                        chain(V.tensor_tensor(cfac.rearrange("p (r t j) -> p r t j", r=2, j=4)[:, par],
                                              cst.rearrange("p (r t j) -> p r t j", r=2, j=4)[:, par],
                                              ngt[:].rearrange("p t (j r b) -> p r b t j", j=4, r=2)[:, par, 0], ALU.mult))
                    chain(V.tensor_tensor(pc, pc, bc(cfac), ALU.mult))
                    for par in range(2):
                        v = Pc[:, par].rearrange("p (t j) c -> p t j c", j=4)
                        ins = V.tensor_tensor(v, v, cok[:].rearrange("p t (o c) -> p t o c", o=1).broadcast_to([P, NT, 4, 32]), ALU.mult)
                    ins.then_inc(S["cprob"], 1)

                    def maxima(u):
                        for i in range(NT):
                            dve.wait_ge(S["score"], 4 * u + i + 1)
                            ins = V.tensor_reduce(att[:, 0, u % 2, i:i + 1], ps[:, i, 0:(i + 1) * P], AX, ALU.max)
                        chain(ins)
                        V.tensor_scalar(att[:, 0, u % 2, :], att[:, 0, u % 2, :], -0.125, None, ALU.mult).then_inc(S["nmax"], 1)

                    def scale_probs(u):
                        h, br = divmod(u, 2)
                        dve.wait_ge(S["exp"], 4 * u + 4)
                        a = att[:, 1, u % 2, :]
                        chain(V.reciprocal(a, a))
                        chain(V.tensor_tensor(a, a, ngt[:, :, 3 * h + 1 + br], ALU.mult))
                        for i in range(NT):
                            o0, n = i * (i + 1) // 2 * P, (i + 1) * P
                            ins = V.tensor_scalar(prob[u % 2][:, o0:o0 + n], prob[u % 2][:, o0:o0 + n], a[:, i:i + 1], None, ALU.mult)
                        ins.then_inc(S["pscaled"], 1)

                    def recurrence(u):
                        t = u // 2
                        if u % 2 == 0:
                            dve.wait_ge(S["wS"], t + 1)
                            V.tensor_tensor(vnew, vb[:, t, :], ps[:, 7, 0:GW], ALU.subtract).then_inc(S["vnew"], 1)
                            return
                        dve.wait_ge(S["oS"], t + 1)
                        V.tensor_copy(og[:, t, :], ps[:, 7, 256:512])
                        for j in range(2):
                            for par in range(2):
                                r = slice(par * HEAD, (par + 1) * HEAD)
                                ins = V.scalar_tensor_tensor(out=state[r, j, r], in0=state[r, j, r], scalar=glc[r, t, j:j + 1],
                                                             in1=ps[r, 7, j * P + par * HEAD:j * P + (par + 1) * HEAD],
                                                             op0=ALU.mult, op1=ALU.add)
                        ins.then_inc(S["state"], 1)

                    def gdn_finish():
                        dve.wait_ge(S["osq"], 1)
                        V.tensor_reduce(st[:, 0, 0:16], zt.rearrange("p t (h d) -> p (t h) d", d=HEAD), AX, ALU.add
                                        ).then_inc(S["ored"], 1)
                        dve.wait_ge(S["ored"], 1)
                        chain(V.tensor_scalar(st[:, 1, 0:16], st[:, 0, 0:16], 1.0 / HEAD, EPS, ALU.mult, ALU.add))
                        rsqrt(st[:, 2, 0:16], st[:, 1, 0:16], st[:, 3, 0:16])
                        o3 = og.rearrange("p t (h d) -> p (t h) d", d=HEAD)
                        chain(V.tensor_tensor(o3, o3, per_head(st[:, 2, 0:16], 16), ALU.mult))
                        chain(V.tensor_tensor(o3, o3, gng[:].rearrange("p (o d) -> p o d", o=1).broadcast_to([P, 16, HEAD]), ALU.mult))
                        dve.wait_ge(S["zth"], 1)
                        chain(V.scalar_tensor_tensor(out=zt, in0=zt, scalar=1.0, in1=z, op0=ALU.add, op1=ALU.mult))
                        V.scalar_tensor_tensor(out=og, in0=og, scalar=0.5, in1=zt, op0=ALU.mult, op1=ALU.mult).then_inc(S["og"], 1)

                    def lo_part(dst, full, hi, done):
                        V.tensor_tensor(dst, full, hi.bitcast(F32), ALU.subtract).then_inc(done, 1)

                    maxima(0)
                    for u in range(2 * NH):
                        scale_probs(u)
                        if u < 2 * NT:
                            recurrence(u)
                        if u == 2 * NT - 1:
                            dve.wait_ge(S["state"], NT)
                            dve.nop().then_inc(S["oall"], 1)
                        if u == OG_UNIT:
                            dve.wait_ge(S["mixg_hi"], 1)
                            lo_part(alo[:, MIX_LO[0], :], ps[:, 7, :], ahi[:, 0, :], S["mixg_lo"])
                        if u + 1 < 2 * NH:
                            maxima(u + 1)
                        if u == OG_UNIT - 1:
                            gdn_finish()
                            for m in range(2):
                                dve.wait_ge(S["mixc_hi"], m + 1)
                                lo_part(alo[:, MIX_LO[6 + m], :], ccb[:, m, :], ahi[:, 6 + m, :], S["mixc_lo"])
                        if u == OG_UNIT + 1:
                            dve.wait_ge(S["mixg_hi"], 2)
                            lo_part(alo[:, MIX_LO[1], :], ps[:, 7, :], ahi[:, 1, :], S["mixg_lo"])
                        if u % 4 == 3:
                            dve.wait_ge(S["mix_hi"], u // 4 + 1)
                            lo_part(alo[:, MIX_LO[2 + u // 4], :], ps[:, 6, :], ahi[:, 2 + u // 4, :], S["mix_lo"])

                    for c in range(N_OUT):
                        for t in range(NT):
                            dve.wait_ge(S["mm"], mm_count(N_IN + c - 1) + t + 1)
                            xs = x[:, t, c * 256:(c + 1) * 256]
                            V.tensor_tensor(xs, ps[:, t, 0:256], xs, ALU.add).then_inc(S["x_res"], 1)
                    norm("1", fn)
                    for f in range(2):
                        for i in range(FT):
                            c, cnt = FFN0 + f * PER_HALF + i, f * FT + i
                            dve.wait_ge(S["silu"], cnt + 1)
                            dve.wait_ge(S["mm"], mm_count(c))
                            if cnt >= 2:
                                dve.wait_ge(S["a_lo"], cnt - 1)
                            V.tensor_tensor(ft[:, 2 + cnt % 2, :], ps[:, 2 * (i % 2) + 1, :], ft[:, cnt % 2, :], ALU.mult
                                            ).then_inc(S["up_mul"], 1)
                            dve.wait_ge(S["a_hi"], cnt + 1)
                            lo_part(alo[:, i, :], ft[:, 2 + cnt % 2, :], ahi[:, i, :], S["a_lo"])
                        for ch in range(2):
                            c = FFN0 + f * PER_HALF + FT + ch * 3 + 2
                            for t in range(NT):
                                dve.wait_ge(S["mm"], mm_count(c - 1) + t + 1)
                                xs = x[:, t, ch * 512:(ch + 1) * 512]
                                V.tensor_tensor(xs, ps[:, (4 if ch == 0 else 0) + t, :], xs, ALU.add).then_inc(S["x_down"], 1)
            clear()

        with nc.Block() as block:
            @block.sync
            def _(sp):
                sp.dma_start(out[0].rearrange("(t p) d -> p t d", p=P), x[:]).then_inc(S["stored"], 16)
                sp.wait_ge(S["stored"], 16)
                sp.wait_ge(prefetched, 32 * (DEPTH + 1))


_INS = ["x", "positions", "attn_norm", "w_in", "gdn_conv_w", "gdn_a_log", "gdn_dt_bias", "gdn_norm", "nsa_q_norm",
        "nsa_k_norm", "nsa_cmp_pe", "nsa_cmp_w1", "nsa_cmp_w2", "conv_w", "w_out", "ffn_norm", "w_gate_up", "w_down"]


def kernel(**inputs):
    import numpy as _np
    import concourse.bacc as _bacc
    from concourse import mybir as _mybir
    from concourse.bass_utils import run_bass_kernel_spmd as _run

    nc = _bacc.Bacc("TRN2", target_bir_lowering=False, num_devices=1)
    arrays, aps = {}, {}
    for name in _INS:
        a = _np.ascontiguousarray(inputs[name])
        arrays[f"in_{name}"] = a
        aps[name] = nc.dram_tensor(f"in_{name}", a.shape, _mybir.dt.from_np(a.dtype), kind="ExternalInput").ap()
    out = nc.dram_tensor("out", inputs["x"].shape, F32, kind="ExternalOutput").ap()
    trunk(nc, aps, out)
    r = _run(nc, [arrays], core_ids=[0])
    return r.results[0]["out"]
```

```python
from contextlib import ExitStack

import numpy as np

import concourse.bass as bass
from concourse import mybir

F32 = mybir.dt.float32
F32R = mybir.dt.float32r
BF16 = mybir.dt.bfloat16
I32 = mybir.dt.int32
ALU = mybir.AluOpType
ACT = mybir.ActivationFunctionType
AX = mybir.AxisListType.X

P = 128
EPS = 1e-6
NEG = -1e30
HEAD = 64
CMP_STRIDE, CMP_LEN = 16, 32
ROPE_THETA = 500000.0
ROT = HEAD // 4
HALF = ROT // 2
SLOT = 280
N_PARAMS = 16
LAG_INVERT, LAG_SCALE, LAG_TRANSPOSE, LAG_EVACUATE, LAG_PV = 1, 1, 3, 3, 5
CMP_TICKS = (11, 13)
RECUR_TICK = 15
RECUR_PERIOD = 6
RECUR_SECOND = 3
OG_TICK = 40
RSQRT_SEED = 1597463007.0


class Semaphores(dict):

    def __init__(self, nc, ctx):
        self.nc, self.ctx = nc, ctx

    def __missing__(self, name):
        self[name] = self.ctx.enter_context(self.nc.semaphore(name))
        return self[name]


class Chain:

    def __init__(self, engine, sem):
        self.engine, self.sem, self.n = engine, sem, 0

    def __call__(self, instruction):
        self.n += 1
        instruction.then_inc(self.sem, 1)
        self.engine.wait_ge(self.sem, self.n)


def trunk(nc, A, out):
    T, D = A["x"].shape[1:]
    DEPTH = A["w_in"].shape[0]
    DFF = A["w_down"].shape[1]
    NT, KD = T // P, D // P
    GH, NH, NG = D // 4 // HEAD, D // 2 // HEAD, 2
    GW, NW, KW = GH * HEAD, NH * HEAD, NG * HEAD
    NC = T // CMP_STRIDE - 1
    FT = DFF // P // 2
    assert (T, D, GH, NH) == (512, 1024, 4, 8) and FT * 2 * P == DFF

    o = np.cumsum([0, GW, GW, GW, GW, GH, GH, NW] + [KW] * 6 + [3 * NH, GW, GW, GW]).tolist()
    GQ, GK, GV, GZ, GB, GA, NQ, KC, VC, KS, VS, KWN, VWN, NGT, CB, CC, CX = o[:17]
    CHUNKS = [("gq", GQ, 256, "C"), ("gk", GK, 256, "C"), ("gv", GV, 256, "C"),
              ("zg", GZ, 264, "T"), ("kvs", KS, 256, "T"), ("kvw", KWN, 280, "T"),
              ("cmp", KC, 256, "C"), ("cc", CC, 256, "C"), ("nq0", NQ, 256, "T"), ("nq1", NQ + 256, 256, "T"),
              ("cx", CX, 256, "C"), ("cb", CB, 256, "C")]
    N_IN = len(CHUNKS)
    N_OUT = D // 256
    DOWN = [(0, 4), (4, 4), (8, FT - 8)]
    PER_HALF = FT + 2 * len(DOWN)
    FFN0 = N_IN + N_OUT
    N_CHUNKS = FFN0 + 2 * PER_HALF
    GROUPS = [(c, g, "dve" if CHUNKS[c][0] in ("cx", "cb") else "act")
              for c in range(N_IN) for g in range(2 if CHUNKS[c][3] == "C" else NT)]
    IN_BANKS = 3

    def emptied(n):
        e = GROUPS[n][2]
        return e, sum(1 for x in GROUPS[:n + 1] if x[2] == e)

    with ExitStack() as ctx:
        def sb(name, shape, dt=F32):
            return ctx.enter_context(nc.sbuf_tensor(name, shape, dt))

        ctx.enter_context(nc.allow_non_contiguous_dma(reason="small transposed parameter loads"))
        S = Semaphores(nc, ctx)
        prefetched = ctx.enter_context(nc.semaphore("prefetched"))

        x = sb("x_tok", [P, NT, D])
        hhi, hlo = sb("hT_hi", [P, KD, T], F32R), sb("hT_lo", [P, KD, T], F32R)
        raw = sb("w_raw", [P, 2, KD * SLOT])
        whi, wlo = sb("w_hi", [P, 2, KD * SLOT], F32R), sb("w_lo", [P, 2, KD * SLOT], F32R)
        ident, tri = sb("ident", [P, P]), sb("tri", [P, P])
        identb, negm = sb("identb", [P, P], BF16), sb("negm", [P, P], BF16)
        below, offblk = sb("below", [P, P], BF16), sb("offblk", [P, P], BF16)
        ones = sb("ones", [P, P])
        cneg, cok = sb("cneg", [P, NT, 32], BF16), sb("cok", [P, NT, 32], BF16)
        cossin = sb("cossin", [P, 2, NT, HALF])
        an, fn = sb("an", [P, KD]), sb("fn", [P, KD])
        cw, scw = sb("cw", [P, 6, 4]), sb("scw", [P, 2, 3])
        alog, dtb = sb("alog", [P, GH]), sb("dtb", [P, GH])
        gng, qg, kg = sb("gng", [P, HEAD]), sb("qg", [P, HEAD]), sb("kg", [P, 3, HEAD])
        pe_c = sb("pe_c", [P, 2, 16])
        w2c = sb("w2c", [HEAD, 2, HEAD])
        st = sb("st", [P, 9, 32])
        gbuf = sb("gbuf", [P, NT, 8])
        gsc = sb("gsc", [P, 9, NT * GH])
        ngt = sb("ngt", [P, NT, 3 * NH])
        peb = sb("peb", [HEAD, 2])
        vcr = sb("vcr", [P, HEAD])
        ktmp = sb("rope_k", [P, 3, NT * NG * HALF])
        kcT = sb("kcT", [P, NG, 2, 32])
        state = sb("state", [P, 2, P])
        glc = sb("glc", [P, NT, 2])
        att = sb("att", [P, 2, 8])
        ffn = ExitStack()
        ahi = ffn.enter_context(nc.sbuf_tensor("aT_hi", [P, FT, T], F32R))
        alo = ffn.enter_context(nc.sbuf_tensor("aT_lo", [P, FT, T], F32R))
        ft = ffn.enter_context(nc.sbuf_tensor("ffn_tmp", [P, 4, T], F32))
        ffn.close()
        arena = sb("arena", [P, 24584])
        ps = ctx.enter_context(nc.psum_tensor("ps", [P, 8, 512], F32))

        def at(off, *shape):
            v = arena[:, off:off + int(np.prod(shape))]
            if len(shape) == 2:
                return v.rearrange("p (a b) -> p a b", a=shape[0])
            if len(shape) == 3:
                return v.rearrange("p (a b c) -> p a b c", a=shape[0], b=shape[1])
            if len(shape) == 4:
                return v.rearrange("p (a b c d) -> p a b c d", a=shape[0], b=shape[1], c=shape[2])
            return v

        hn = at(15360, NT, D)
        junk = at(19456, D)
        gtm = at(0, NT, 3 * GW)
        cM, cMT, cM2, cM2T, cM4T, cZ1 = (at(512 * i, GH, P) for i in range(6))
        qT, kT, qdT = (at(3072 + 1024 * i, 2, T) for i in range(3))
        L = at(6144, NT * GH, P)
        x2 = at(0, 2, 2, T)
        qd = at(6144, NT, GW)
        vb, kdec = at(8192, NT, GW), at(9216, NT, GW)
        dA, dB = at(10240, GH, P), at(10752, GH, P)
        wT = at(10240, 2, T)
        TD, TDT = at(11264, NT * GH, P), at(13312, NT * GH, P)
        w1c = at(3072, 2, 16, HEAD)
        hid = at(10240, 3, 2 * 2 * NC)[0:HEAD]
        kcn = at(10240 + 12 * NC, 2, P)[0:32]
        gpre = at(15360, 2, 516)
        gcm = at(15360 + 1032, 2, T)
        ccb = at(15360, 2, T)
        cpre = at(15360 + 1024, 2, 514)
        kbe = at(17416, NT, GW)
        og = at(17416, NT, GW)
        qkT = at(18440, NT * GH, P)
        Dm, Ti = at(20488, 16, 16), at(20488 + 256, 16, 16)
        Tt, dtmp = at(20488 + 512, 16, 16), at(20488 + 768, 16, 16)
        trig = at(13312, 2, GH * P)
        nq = at(3072, NT, NW)
        z = at(21512, NT, GW)
        kv = at(22536, NT, 4 * KW)
        qnT = at(0, 4, T)
        Pc, PcT = at(20488, 2, 16, 32), at(4096, 2, T)
        vnew = at(3072, GW)
        jq = at(20488, 2, NW)
        rot = at(20488, 3, NT * NH * HALF)
        zt = at(16384, NT, GW)
        prob = [at(11264 + 512 * i, T) for i in range(5)]
        pT = [at(13824 + 512 * i, T) for i in range(3)]
        qst = hhi
        kst = hlo
        MIX_LO = [0, 5, 1, 2, 3, 4, 6, 7]
        d_in = nc.dram_tensor("diag_in", [8, 16, 16, 16], F32).ap()
        d_out = nc.dram_tensor("diag_out", [2, 8, 16, 16, 16], F32).ap()

        def slot(buf, c, kt, w):
            return buf[:, c % 2, 0:kt * w].rearrange("p (k n) -> p k n", k=kt)

        def chunk_shape(c):
            if c < N_IN:
                return KD, CHUNKS[c][2]
            if c < FFN0:
                return KD, 256
            i = (c - FFN0) % PER_HALF
            return (KD, 256) if i < FT else (DOWN[(i - FT) % 3][1], 512)

        def norm_square(act, t, sem):
            if t:
                act.wait_ge(sem, t)
            nc.scalar.activation(junk, x[:, t, :], ACT.Square, accum_out=st[:, 8, t:t + 1]).then_inc(sem, 1)

        def rsqrt(chain, y, v, t):
            V = nc.vector
            chain(V.tensor_scalar(y.bitcast(I32), v.bitcast(I32), -0.5, RSQRT_SEED, ALU.mult, ALU.add))
            for _ in range(3):
                chain(V.tensor_tensor(t, y, y, ALU.mult))
                chain(V.scalar_tensor_tensor(out=t, in0=t, scalar=-0.5, in1=v, op0=ALU.mult, op1=ALU.mult))
                chain(V.scalar_tensor_tensor(out=y, in0=t, scalar=1.5, in1=y, op0=ALU.add, op1=ALU.mult))

        def norm_scale(dve, chain, tiles, squares, done):
            t0, t1 = tiles
            dve.wait_ge(squares, t1)
            a, v, y, w = (st[:, 8, 4 * i + t0:4 * i + t1] for i in range(4))
            chain(nc.vector.tensor_scalar(v, a, 1.0 / D, EPS, ALU.mult, ALU.add))
            rsqrt(chain, y, v, w)
            for t in range(t0, t1):
                nc.vector.tensor_scalar(hn[:, t, :], x[:, t, :], y[:, t - t0:t - t0 + 1], None, ALU.mult).then_inc(done, 1)

        with nc.Block() as block:
            @block.sync
            def _(sp):
                sp.dma_start(st[:, 0, 0:NT].bitcast(I32), A["positions"].rearrange("o (t p) -> p (o t)", p=P)
                             ).then_inc(S["pos_in"], 16)
                for t in range(NT):
                    sp.dma_start(x[:, t, :], A["x"][0, t * P:(t + 1) * P, :]).then_inc(S[f"x_in{t}"], 16)
                for c in range(2):
                    _, c0, w, _ = CHUNKS[c]
                    sp.dma_start(slot(raw, c, KD, w), A["w_in"][0].rearrange("(k p) n -> p k n", p=P)[:, :, c0:c0 + w]
                                 ).then_inc(prefetched, 16)

            @block.gpsimd
            def _(pool):
                chain = Chain(pool, S["pool_chain"])

                def select(t, base, pattern, cm, op, fill):
                    chain(nc.gpsimd.affine_select(out=t, in_=t, compare_op=op, fill=fill, base=base,
                                                  pattern=pattern, channel_multiplier=cm))

                for t, v in ((ident, 0.0), (identb, 0.0), (tri, 1.0), (below, 1.0), (offblk, 1.0), (negm, 0.0),
                             (ones, 1.0), (cneg, 0.0), (cok, 1.0), (state, 0.0), (kcT, 0.0)):
                    chain(nc.gpsimd.memset(t[:], v))
                for t in (ident, identb):
                    select(t[:], 0, [[-1, P]], 1, ALU.not_equal, 1.0)
                select(tri[:], 0, [[1, P]], -1, ALU.is_ge, 0.0)
                select(below[:], -1, [[-1, P]], 1, ALU.is_ge, 0.0)
                select(negm[:], 0, [[-1, P]], 1, ALU.is_ge, NEG)
                select(offblk[:].rearrange("p (b j) -> p b j", b=8), -16, [[-16, 8], [0, 16]], 1, ALU.is_ge, 0.0)
                for m, fill in ((cneg, NEG), (cok, 0.0)):
                    select(m[:], -(CMP_LEN - 1), [[P, NT], [-CMP_STRIDE, 32]], 1, ALU.is_ge, fill)

            @block.vector
            def _(dve):
                chain = Chain(dve, S["dve_chain"])
                dve.wait_ge(S["pos_in"], 16)
                chain(nc.vector.tensor_copy(st[:, 1, 0:NT], st[:, 0, 0:NT].bitcast(I32)))
                ang, k, r = (st[:, 2 + i, 0:NT * HALF].rearrange("p (t f) -> p t f", t=NT) for i in range(3))
                for f in range(HALF):
                    inv = float(np.float32(np.float64(np.float32(ROPE_THETA)) ** (-2.0 * f / ROT)))
                    chain(nc.vector.tensor_scalar(ang[:, :, f], st[:, 1, 0:NT], inv, None, ALU.mult))
                two_pi = 2 * np.pi
                c1 = 6.28125
                c2 = float(np.float32(np.floor((two_pi - c1) * 2 ** 20) / 2 ** 20))
                c3 = float(np.float32(two_pi - c1 - c2))
                magic = 12582912.0
                for i, shift in ((0, np.pi / 2), (1, 0.0)):
                    chain(nc.vector.tensor_scalar(k, ang, float(1 / two_pi), float(shift / two_pi), ALU.mult, ALU.add))
                    chain(nc.vector.tensor_scalar(k, k, magic, None, ALU.add))
                    chain(nc.vector.tensor_scalar(k, k, magic, None, ALU.subtract))
                    chain(nc.vector.tensor_copy(r, ang))
                    for cst in (c1, c2, c3):
                        chain(nc.vector.scalar_tensor_tensor(out=r, in0=k, scalar=-cst, in1=r, op0=ALU.mult, op1=ALU.add))
                    chain(nc.vector.tensor_scalar(r, r, float(shift), 3.1415925, ALU.add, ALU.min))
                    chain(nc.vector.tensor_scalar(cossin[:, i], r, -3.1415925, None, ALU.max))
                dve.nop().then_inc(S["angles"], 1)
                norm_scale(dve, chain, (0, NT), S["ssq_first"], S["hn_first"])

            @block.scalar
            def _(act):
                for t in range(NT):
                    act.wait_ge(S[f"x_in{t}"], 16)
                    norm_square(act, t, S["ssq_first"])
                act.wait_ge(S["angles"], 1)
                nc.scalar.activation(cossin[:], cossin[:], ACT.Sin).then_inc(S["rope"], 1)
                act.wait_ge(S["rope"], 1)

        def clear():
            nc.all_engine_barrier()
            ids = sorted(s.num for s in S.values())
            assert ids == list(range(ids[0], ids[-1] + 1))
            nc.gpsimd.sem_clear(range(ids[0], ids[-1] + 1))
            nc.all_engine_barrier()

        clear()

        def mm_count(c):
            n = 0
            for i in range(c + 1):
                if i < N_IN:
                    n += 2 if CHUNKS[i][3] == "C" else NT
                elif i < FFN0:
                    n += NT
                else:
                    n += 2 if (i - FFN0) % PER_HALF < FT else NT
            return n

        def loads(c):
            return sum(2 if i >= FFN0 and (i - FFN0) % PER_HALF < FT else 1 for i in range(2 + c % 2, c + 1, 2))

        HOP_GROUP = 24
        Q_BANKS = (6, 7, 0, 1)
        N_ITEMS = 2 * NH * NT

        with nc.Fori(0, DEPTH) as l:
            with nc.Block() as block:
                @block.sync
                def _(sp):
                    for dst, src in ((an[:], A["attn_norm"][l].rearrange("(k p) -> p k", p=P)),
                                     (fn[:], A["ffn_norm"][l].rearrange("(k p) -> p k", p=P))):
                        sp.dma_start(dst, src).then_inc(S["norm_gains"], 16)

                    def row(name, n):
                        return A[name][l].rearrange("(o n) -> o n", o=1).broadcast_to([P, n])

                    params = [
                        (w2c[:], A["nsa_cmp_w2"][l].rearrange("k i d -> i k d")),
                        (scw[:, 0], A["conv_w"][l].rearrange("k (j p) -> j p k", p=P)[0]),
                        (scw[:, 1], A["conv_w"][l].rearrange("k (j p) -> j p k", p=P)[1]),
                        (alog[:], row("gdn_a_log", GH)), (dtb[:], row("gdn_dt_bias", GH)),
                        (gng[:], row("gdn_norm", HEAD)), (qg[:], row("nsa_q_norm", HEAD)),
                        (kg[:].rearrange("p a d -> p (a d)"),
                         A["nsa_k_norm"][l].rearrange("(o a) d -> o (a d)", o=1).broadcast_to([P, 3 * HEAD])),
                    ]
                    params += [(cw[:, j], A["gdn_conv_w"][l].rearrange("k (j p) -> j p k", p=P)[j]) for j in range(6)]
                    params += [(pe_c[:, k], A["nsa_cmp_pe"][l, k].rearrange("(m r) d -> (r d) m", r=2)) for k in range(2)]
                    assert len(params) == N_PARAMS
                    for dst, src in params:
                        sp.dma_start(dst, src).then_inc(S["params"], 16)

                    for c in range(2, N_CHUNKS):
                        sp.wait_ge(S["w_lo"], c - 1)
                        kt, w = chunk_shape(c)
                        if c < N_IN:
                            src = A["w_in"][l].rearrange("(k p) n -> p k n", p=P)[:, :, CHUNKS[c][1]:CHUNKS[c][1] + w]
                            dst = slot(raw, c, kt, w)
                        elif c < FFN0:
                            n0 = (c - N_IN) * 256
                            src = A["w_out"][l].rearrange("(k p) n -> p k n", p=P)[:, :, n0:n0 + 256]
                            dst = slot(raw, c, kt, w)
                        else:
                            f, i = divmod(c - FFN0, PER_HALF)
                            if i < FT:
                                n0 = (f * FT + i) * P
                                src = A["w_gate_up"][l].rearrange("(k p) n -> p k n", p=P)
                                sp.dma_start(slot(raw, c, kt, w)[:, :, 0:P], src[:, :, n0:n0 + P]).then_inc(S[f"w_in{c % 2}"], 16)
                                src = src[:, :, DFF + n0:DFF + n0 + P]
                                dst = slot(raw, c, kt, w)[:, :, P:2 * P]
                            else:
                                ch, (k0, _) = (i - FT) // 3, DOWN[(i - FT) % 3]
                                r0 = (f * FT + k0) * P
                                src = A["w_down"][l][r0:r0 + kt * P].rearrange("(k p) n -> p k n", p=P)[:, :, ch * 512:ch * 512 + 512]
                                dst = slot(raw, c, kt, w)
                        sp.dma_start(dst, src).then_inc(S[f"w_in{c % 2}"], 16)
                        if c == 8:
                            sp.wait_ge(S["A"], NT)
                            for b in range(8):
                                sp.dma_start(d_in[b].rearrange("q i j -> i q j"), L[16 * b:16 * b + 16, :, 16 * b:16 * b + 16]
                                             ).then_inc(S["d_in"], 16)
                            sp.wait_ge(S["d_in"], 128)
                            sp.dma_start(Dm.rearrange("p i j -> p (i j)"), d_in.rearrange("b q i j -> (b q) (i j)")
                                         ).then_inc(S["Dm"], 16)
                            sp.wait_ge(S["gram"], NT)
                            for k in range(2):
                                sp.dma_start(w1c[:, k], A["nsa_cmp_w1"][l, k].rearrange("(m p) j -> p m j", p=P)
                                             ).then_inc(S["w1"], 16)
                        if c == 9:
                            sp.wait_ge(S["Tt"], 1)
                            for s, src in enumerate((Ti, Tt)):
                                sp.dma_start(d_out[s].rearrange("b q i j -> (b q) (i j)"), src.rearrange("p i j -> p (i j)")
                                             ).then_inc(S["d_out"], 16)
                            sp.wait_ge(S["d_out"], 32)
                            sp.wait_ge(S["tdzero"], 1)
                            for s, dst in enumerate((TD, TDT)):
                                for b in range(8):
                                    sp.dma_start(dst[16 * b:16 * b + 16, :, 16 * b:16 * b + 16],
                                                 d_out[s, b].rearrange("q i j -> i q j")).then_inc(S["TD"], 16)
                    for c in range(2):
                        sp.wait_ge(S["w_lo"], N_CHUNKS - 1 + c)
                        _, c0, w, _ = CHUNKS[c]
                        sp.dma_start(slot(raw, c, KD, w),
                                     A["w_in"][(l + 1) % DEPTH].rearrange("(k p) n -> p k n", p=P)[:, :, c0:c0 + w]
                                     ).then_inc(prefetched, 16)

                @block.tensor
                def _(pe):
                    def norm_transposes(tag):
                        def block(k, t):
                            return nc.tensor.transpose(ps[:, k, t * P:(t + 1) * P], hn[:, t, k * P:(k + 1) * P], ident[:])

                        if tag == "1":
                            for t in range(NT):
                                pe.wait_ge(S["hn1"], t + 1)
                                for k in range(4):
                                    mm = block(k, t)
                            mm.then_inc(S["hps1"], 4)
                        for k in range(4 if tag == "1" else 0, KD):
                            if tag == "1" and k == 4:
                                pe.wait_ge(S["x_res"], 16)
                            for t in range(NT):
                                mm = block(k, t)
                            mm.then_inc(S["hps" + tag], 1)

                    def first_group(out_ap, a, b, tag, lo_ready):
                        pe.wait_ge(S["hlo" + tag], 1)
                        for k in range(KD):
                            pe.wait_ge(S["hhi" + tag], k + 1)
                            nc.tensor.matmul(out_ap, a(0, k), b(0, k), start=k == 0, stop=False)
                        for k in range(KD):
                            pe.wait_ge(S["hlo" + tag], k + 1)
                            nc.tensor.matmul(out_ap, a(0, k), b(1, k), start=False, stop=False)
                        pe.wait_ge(S["w_lo"], lo_ready)
                        three_pass(out_ap, a, b, 2, range(KD), False, True, S["mm"])

                    def three_pass(out_ap, a, b, part, kts, first, last, sem=None):
                        ab, bb = ((0, 0), (0, 1), (1, 0))[part]
                        for i, k in enumerate(kts):
                            mm = nc.tensor.matmul(out_ap, a(ab, k), b(bb, k), start=first and i == 0,
                                                  stop=last and i == len(kts) - 1)
                        if sem is not None:
                            mm.then_inc(sem, 1)

                    def in_group(n, part):
                        c, g, _ = GROUPS[n]
                        _, _, w, kind = CHUNKS[c]
                        if n == 0:
                            if part == 0:
                                pe.wait_ge(S["w_hi"], 1)
                                first_group(ps[:, 0, :], lambda b, k: (slot(whi, 0, KD, w), slot(wlo, 0, KD, w))[b][:, k, 0:P],
                                            lambda b, k: (hhi, hlo)[b][:, k, :], "0", 1)
                            return
                        if part == 0:
                            if g == 0:
                                pe.wait_ge(S["w_lo"], c + 1)
                            if n >= IN_BANKS:
                                e, v = emptied(n - IN_BANKS)
                                pe.wait_ge(S["ev_" + e], v)
                        W = (slot(whi, c, KD, w), slot(wlo, c, KD, w))
                        h = (hhi, hlo)
                        bank = n % IN_BANKS
                        done = S["mm"] if part == 2 else None
                        if kind == "C":
                            three_pass(ps[:, bank, :], lambda b, k: W[b][:, k, g * P:(g + 1) * P], lambda b, k: h[b][:, k, :],
                                       part, range(KD), part == 0, part == 2, done)
                        else:
                            three_pass(ps[:, bank, 0:w], lambda b, k: h[b][:, k, g * P:(g + 1) * P], lambda b, k: W[b][:, k, :],
                                       part, range(KD), part == 0, part == 2, done)

                    def cmp_first():
                        pe.wait_ge(S["ev_act"], 20)
                        pe.wait_ge(S["w1"], 32)
                        pe.wait_ge(S["A"], NT)
                        pe.wait_ge(S["params"], 16 * N_PARAMS)
                        for k in range(2):
                            for m in range(16):
                                nc.tensor.matmul(ps[0:HEAD, 3, k * P:k * P + 2 * NC].rearrange("p (g n) -> p g n", g=2),
                                                 w1c[:, k, m, :], x2[:, k, :, 2 * m:2 * m + CMP_STRIDE * (NC - 1) + 1:CMP_STRIDE],
                                                 start=(k == 0 and m == 0), stop=(m == 15), skip_group_check=True)
                            for m in range(16):
                                mm = nc.tensor.matmul(ps[0:HEAD, 3, k * P + 2 * NC:k * P + 2 * NC + 1], w1c[:, k, m, :],
                                                      pe_c[:, k, m:m + 1], start=False, stop=(m == 15), skip_group_check=True)
                        mm.then_inc(S["cmp"], 1)

                    def cmp_second():
                        pe.wait_ge(S["cmp_hid"], 1)
                        for k in range(2):
                            for g in range(NG):
                                mm = nc.tensor.matmul(ps[0:NC, 7, (k * 2 + g) * HEAD:(k * 2 + g + 1) * HEAD],
                                                      hid[:, 0, k * 2 * NC + g * NC:k * 2 * NC + (g + 1) * NC], w2c[:, k, :],
                                                      start=True, stop=True)
                        mm.then_inc(S["cmp"], 1)

                    def cmp_third():
                        pe.wait_ge(S["cmp_kn"], 1)
                        nc.tensor.transpose(ps[:, 7, 0:NC], kcn[0:NC, 0, :], ident[0:NC, 0:NC]).then_inc(S["cmp"], 1)

                    def gdn_transpose(j):
                        pe.wait_ge(S["conv"], j + 1)
                        if j >= 3:
                            pe.wait_ge(S["gtm"], j - 2)
                        for t in range(NT):
                            mm = nc.tensor.transpose(ps[:, 3 + j % 3, t * P:(t + 1) * P], gcm[:, j % 2, t * P:(t + 1) * P], ident[:])
                        mm.then_inc(S["gtr"], 1)

                    def gdn_back(i, bank):
                        pe.wait_ge(S["qdec"] if i >= 4 else S["qkn"], 1)
                        if i == 0:
                            pe.wait_ge(S["gtm"], 6)
                        if i == 4:
                            pe.wait_ge(S["scan"], 1)
                        if i == 5:
                            pe.wait_ge(S["gT"], 1)
                        for t in range(NT):
                            src = qd[:, t, (i % 2) * P:(i % 2 + 1) * P] if i >= 4 else gtm[:, t, i * P:(i + 1) * P]
                            mm = nc.tensor.transpose(ps[:, bank, t * P:(t + 1) * P], src, ident[:])
                        mm.then_inc(S["gback"], 1)

                    def gdn_cumsum():
                        pe.wait_ge(S["g"], 1)
                        nc.tensor.matmul(ps[:, 7, 0:16], tri[:], gsc[:, 0, :], start=True, stop=True)
                        nc.tensor.matmul(ps[:, 7, 16:32], ones[:], gsc[:, 0, :], start=False, stop=True,
                                         skip_group_check=True).then_inc(S["gsum"], 1)

                    def gdn_grams(t):
                        pe.wait_ge(S["trig"], t + 1)
                        pe.wait_ge(S["gT"], 6)
                        if t >= 1:
                            pe.wait_ge(S["dec"], t)
                        nc.tensor.matmul(ps[:, 7, :], ones[:], trig[:, t % 2, :], start=True, stop=True).then_inc(S["gr"], 1)
                        if t >= 1:
                            pe.wait_ge(S["A"], t)
                        cols = slice(t * P, (t + 1) * P)
                        for par in range(2):
                            rows = slice(par * HEAD, (par + 1) * HEAD)
                            for j in range(2):
                                nc.tensor.matmul(ps[:, 3 + par, j * P:(j + 1) * P], kT[rows, j, cols], kT[rows, j, cols],
                                                 start=(j == 0), stop=True, skip_group_check=True)
                        for par in range(2):
                            rows = slice(par * HEAD, (par + 1) * HEAD)
                            for j in range(2):
                                mm = nc.tensor.matmul(ps[:, 5 + par, j * P:(j + 1) * P], kT[rows, j, cols], qT[rows, j, cols],
                                                      start=(j == 0), stop=True, skip_group_check=True)
                        mm.then_inc(S["gram"], 1)

                    def batch(bank, lhs, rhs):
                        for h in range(GH):
                            mm = nc.tensor.matmul(ps[:, bank, h * P:(h + 1) * P], lhs(h), rhs(h), start=True, stop=True)
                        return mm

                    def hop(s):
                        t, i = divmod(s, 7)
                        q = t * GH
                        if i == 0:
                            if t == 0:
                                pe.wait_ge(S["Lmask"], 1)
                                pe.wait_ge(S["kcT"], 1)
                                pe.wait_ge(S["TD"], 256)
                                pe.wait_ge(S["A"], 4)
                            else:
                                pe.wait_ge(S["hop_dve"], 6 * t)
                                pe.wait_ge(S["hop_act"], 4 * t)
                            batch(4, lambda h: L[:, q + h, :], lambda h: TDT[:, q + h, :])
                            mm = batch(5, lambda h: TDT[:, q + h, :], lambda h: L[:, q + h, :])
                        elif i == 1:
                            pe.wait_ge(S["hop_dve"], 6 * t + 1)
                            pe.wait_ge(S["hop_act"], 4 * t + 1)
                            batch(6, lambda h: cMT[:, h, :], lambda h: cM[:, h, :])
                            mm = batch(7, lambda h: cM[:, h, :], lambda h: cMT[:, h, :])
                        elif i == 2:
                            pe.wait_ge(S["hop_dve"], 6 * t + 2)
                            pe.wait_ge(S["hop_act"], 4 * t + 2)
                            mm = batch(4, lambda h: cM2[:, h, :], lambda h: cM2T[:, h, :])
                        elif i == 3:
                            pe.wait_ge(S["hop_dve"], 6 * t + 3)
                            mm = batch(5, lambda h: cM4T[:, h, :], lambda h: TD[:, q + h, :])
                        elif i == 4:
                            pe.wait_ge(S["hop_dve"], 6 * t + 4)
                            mm = batch(6, lambda h: cM2T[:, h, :], lambda h: cZ1[:, h, :])
                        elif i == 5:
                            pe.wait_ge(S["hop_dve"], 6 * t + 5)
                            pe.wait_ge(S["hop_pool"], t + 1)
                            mm = batch(7, lambda h: cM[:, h, :], lambda h: cMT[:, h, :])
                        else:
                            pe.wait_ge(S["hop_act"], 4 * t + 3)
                            for h in range(GH):
                                nc.tensor.matmul(ps[:, 3, h * HEAD:(h + 1) * HEAD], cM4T[:, h, :], vb[:, t, h * HEAD:(h + 1) * HEAD],
                                                 start=True, stop=True)
                            for h in range(GH):
                                par, j = h % 2, h // 2
                                mm = nc.tensor.matmul(ps[par * HEAD:(par + 1) * HEAD, 4, j * P:(j + 1) * P],
                                                      kbe[:, t, h * HEAD:(h + 1) * HEAD], cM4T[:, h, :],
                                                      start=True, stop=True)
                        mm.then_inc(S["hop"], 1)

                    norm_transposes("0")
                    slots = 0
                    for n in range(len(GROUPS)):
                        for part in range(3):
                            in_group(n, part)
                            if n >= HOP_GROUP and slots < 7 * NT:
                                hop(slots)
                                slots += 1
                        if 2 <= n <= 7:
                            gdn_transpose(n - 2)
                        if n == 10:
                            for i in range(4):
                                gdn_back(i, 3 + i)
                                if i == 1:
                                    gdn_cumsum()
                        if n == 12:
                            gdn_back(4, 7)
                            gdn_back(5, 3)
                        if 13 <= n <= 16:
                            gdn_grams(n - 13)
                        if n == 20:
                            cmp_first()
                        if n == 21:
                            cmp_second()
                        if n == 23:
                            cmp_third()
                    assert slots == 7 * NT

                    pe.wait_ge(S["qn"], 1)
                    pe.wait_ge(S["hop_act"], 4 * NT)
                    pe.wait_ge(S["hop_dve"], 6 * NT)
                    pe.wait_ge(S["ev_dve"], 4)
                    for j in range(4):
                        for t in range(NT):
                            mm = nc.tensor.transpose(ps[:, j, t * P:(t + 1) * P], nq[:, t, j * P:(j + 1) * P], ident[:])
                        mm.then_inc(S["qnps"], 1)
                    pe.wait_ge(S["kn"], 1)
                    for br in range(2):
                        for t in range(NT):
                            mm = nc.tensor.transpose(ps[:, 4 + br, t * P:(t + 1) * P], kv[:, t, br * 256:br * 256 + P], ident[:])
                        mm.then_inc(S["kps"], 1)
                    pe.wait_ge(S["roped"], 1)
                    for j in range(4):
                        if j >= 2:
                            pe.wait_ge(S["qnT"], j - 1)
                        for t in range(NT):
                            mm = nc.tensor.transpose(ps[:, Q_BANKS[j], t * P:(t + 1) * P], nq[:, t, j * P:(j + 1) * P], ident[:])
                        mm.then_inc(S["qps"], 1)

                    pe.wait_ge(S["qnT"], 4)
                    for j in range(4):
                        for t in range(NT):
                            mm = nc.tensor.matmul(ps[:, 2 + j // 2, (j % 2 * 4 + t) * 64:(j % 2 * 4 + t) * 64 + 63],
                                                  qnT[:, j, t * P:(t + 1) * P], kcT[:, j // 2].rearrange("p r c -> p (r c)")[:, 0:63],
                                                  start=(j % 2 == 0 and t == 0), stop=True, skip_group_check=True)
                        if j % 2:
                            mm.then_inc(S["csc"], 1)

                    def cmp_transpose(par):
                        if par == 0:
                            pe.wait_ge(S["cprob"], 1)
                        else:
                            pe.wait_ge(S["PcT"], 1)
                        for t in range(NT):
                            mm = nc.tensor.transpose(ps[:, 7, t * P:(t + 1) * P],
                                                     Pc[:, par, 4 * t:4 * t + 4, :].rearrange("p j c -> p (j c)"), ident[:])
                        mm.then_inc(S["cpt"], 1)

                    def scores(s):
                        u, i = divmod(s, NT)
                        h, br = divmod(u, 2)
                        g = h // 4
                        if s >= NT:
                            pe.wait_ge(S["exp"], s - NT + 1)
                        elif s == 0:
                            pe.wait_ge(S["klo"], 4)
                            pe.wait_ge(S["qlo"], 4)
                        elif s in (2, 3):
                            pe.wait_ge(S["cadd"], 2 * (s - 1))
                        n = max(256, (i + 1) * P)
                        q_ap = qst[:, h, i * P:(i + 1) * P]
                        nc.tensor.matmul(ps[:, i, 0:n], q_ap, kst[:, br * 2 + g, 0:n], start=True, stop=False)
                        nc.tensor.matmul(ps[:, i, 0:n], q_ap, kst[:, 4 + br * 2 + g, 0:n], start=False, stop=True)
                        nc.tensor.matmul(ps[:, i, i * P:(i + 1) * P], identb[:], negm[:], start=False, stop=True,
                                         skip_group_check=True).then_inc(S["score"], 1)

                    def p_transpose(s):
                        i = s % NT
                        pe.wait_ge(S["pscaled"], s + 1)
                        if s >= 2:
                            pe.wait_ge(S["pTe"], s - 1)
                        for j in range(i + 1):
                            mm = nc.tensor.transpose(ps[:, 4 + s % 2, j * P:(j + 1) * P], prob[s % 5][:, j * P:(j + 1) * P], ident[:])
                        mm.then_inc(S["ptr"], 1)

                    def pv(s):
                        u, i = divmod(s, NT)
                        h, br = divmod(u, 2)
                        pe.wait_ge(S["pTe"], s + 1)
                        if s and s % 16 == 0:
                            pe.wait_ge(S["mix_lo"], s // 16)
                        v0 = br * 256 + P + (h // 4) * HEAD
                        for j in range(i + 1):
                            mm = nc.tensor.matmul(ps[(h % 2) * HEAD:(h % 2 + 1) * HEAD, 6, i * P:(i + 1) * P], kv[:, j, v0:v0 + HEAD],
                                                  pT[s % 3][:, j * P:(j + 1) * P], start=s % 8 == 0, stop=False,
                                                  skip_group_check=True)
                        mm.then_inc(S["pv"], 1)

                    def cmp_pv(h):
                        par, j = h % 2, h // 2
                        if h == 0:
                            pe.wait_ge(S["PcT"], 2)
                        nc.tensor.matmul(ps[par * HEAD:(par + 1) * HEAD, 6, :], vcr[32 * j:32 * j + NC, :],
                                         PcT[32 * j:32 * j + NC, par, :], start=False, stop=True, skip_group_check=True)

                    def recur_first(t):
                        pe.wait_ge(S["state"], t) if t else pe.wait_ge(S["PcT"], 2)
                        for j in range(2):
                            mm = nc.tensor.matmul(ps[:, 7, j * P:(j + 1) * P], wT[:, j, t * P:(t + 1) * P], state[:, j, :],
                                                  start=(j == 0), stop=True, skip_group_check=True)
                        mm.then_inc(S["wS"], 1)

                    def recur_second(t):
                        pe.wait_ge(S["vnew"], t + 1)
                        for j in range(2):
                            nc.tensor.matmul(ps[:, 7, j * P:(j + 1) * P], kdec[:, t, j * P:(j + 1) * P], vnew[:, j * P:(j + 1) * P],
                                             start=(j == 0), stop=True, skip_group_check=True)
                        for j in range(2):
                            nc.tensor.matmul(ps[:, 7, 256 + j * P:256 + (j + 1) * P], qdT[:, j, t * P:(t + 1) * P], state[:, j, :],
                                             start=False, stop=False, skip_group_check=True)
                        for h in range(GH):
                            c0 = 256 + h * HEAD
                            mm = nc.tensor.matmul(ps[:, 7, c0:c0 + HEAD], qkT[:, t * GH + h, :], vnew[:, h * HEAD:(h + 1) * HEAD],
                                                  start=False, stop=True, skip_group_check=True)
                        mm.then_inc(S["oS"], 1)

                    def gdn_out(m):
                        pe.wait_ge(S["og"], 1)
                        if m == 1:
                            pe.wait_ge(S["mixg_lo"], 1)
                        for t in range(NT):
                            mm = nc.tensor.transpose(ps[:, 7, t * P:(t + 1) * P], og[:, t, m * P:(m + 1) * P], ident[:])
                        mm.then_inc(S["ogT"], 1)

                    for tick in range(N_ITEMS + LAG_PV):
                        if tick < N_ITEMS:
                            scores(tick)
                        if tick in CMP_TICKS:
                            cmp_transpose(CMP_TICKS.index(tick))
                        t, step = divmod(tick - RECUR_TICK, RECUR_PERIOD)
                        if 0 <= t < NT and step == 0:
                            recur_first(t)
                        if 0 <= t < NT and step == RECUR_SECOND:
                            recur_second(t)
                        if tick in (OG_TICK + 14, OG_TICK + 17):
                            gdn_out((tick - OG_TICK - 14) // 3)
                        if 0 <= tick - LAG_TRANSPOSE < N_ITEMS:
                            p_transpose(tick - LAG_TRANSPOSE)
                        s = tick - LAG_PV
                        if s >= 0:
                            if s % 16 == 15:
                                cmp_pv(s // 8 - 1)
                                cmp_pv(s // 8)
                            pv(s)

                    pe.wait_ge(S["mixg_lo"], 2)
                    pe.wait_ge(S["mixc_lo"], 2)
                    for c in range(N_IN, FFN0):
                        pe.wait_ge(S["w_lo"], c + 1)
                        W = (slot(whi, c, KD, 256), slot(wlo, c, KD, 256))
                        mix = (lambda k: ahi[:, k, :], lambda k: alo[:, MIX_LO[k], :])
                        for t in range(NT):
                            if c > N_IN:
                                pe.wait_ge(S["x_res"], 4 * (c - N_IN - 1) + t + 1)
                            if c == N_IN and t == 0:
                                ready = [0, 1, 6, 7, 2, 3, 4]
                                for part in range(3):
                                    three_pass(ps[:, 4, 0:256], lambda b, k: mix[b](k)[:, 0:P], lambda b, k: W[b][:, k, :],
                                               part, ready, part == 0, False)
                                pe.wait_ge(S["mix_lo"], 4)
                                for part in range(3):
                                    three_pass(ps[:, 4, 0:256], lambda b, k: mix[b](k)[:, 0:P], lambda b, k: W[b][:, k, :],
                                               part, [5], False, part == 2, S["mm"] if part == 2 else None)
                                continue
                            for part in range(3):
                                three_pass(ps[:, 4 + t, 0:256], lambda b, k: mix[b](k)[:, t * P:(t + 1) * P], lambda b, k: W[b][:, k, :],
                                           part, range(KD), part == 0, part == 2, S["mm"] if part == 2 else None)

                    norm_transposes("1")
                    for f in range(2):
                        for i in range(FT):
                            c, cnt = FFN0 + f * PER_HALF + i, f * FT + i
                            pe.wait_ge(S["w_lo"], c + 1)
                            W = (slot(whi, c, KD, 256), slot(wlo, c, KD, 256))
                            h = (hhi, hlo)
                            for s in range(2):
                                if cnt == 0 and s == 0:
                                    first_group(ps[:, 0, :], lambda b, k: W[b][:, k, 0:P], lambda b, k: h[b][:, k, :], "1", c + 1)
                                    continue
                                if i >= 2:
                                    pe.wait_ge(S["up_mul"] if s else S["silu"], cnt - 1)
                                elif f == 1:
                                    pe.wait_ge(S["x_down"], 4 + 2 * i + s + 1)
                                for part in range(3):
                                    three_pass(ps[:, 2 * (i % 2) + s, :], lambda b, k: W[b][:, k, s * P:(s + 1) * P],
                                               lambda b, k: h[b][:, k, :], part, range(KD), part == 0, part == 2,
                                               S["mm"] if part == 2 else None)
                        for ch in range(2):
                            for q, (k0, kn) in enumerate(DOWN):
                                c = FFN0 + f * PER_HALF + FT + ch * 3 + q
                                pe.wait_ge(S["w_lo"], c + 1)
                                if ch == 0:
                                    pe.wait_ge(S["a_lo"], f * FT + k0 + kn)
                                W = (slot(whi, c, kn, 512), slot(wlo, c, kn, 512))
                                a = (ahi, alo)
                                for t in range(NT):
                                    if q == 0 and f == 1 and ch == 0:
                                        pe.wait_ge(S["x_down"], t + 1)
                                    for part in range(3):
                                        three_pass(ps[:, (4 if ch == 0 else 0) + t, :],
                                                   lambda b, k: a[b][:, k0 + k, t * P:(t + 1) * P], lambda b, k: W[b][:, k, :],
                                                   part, range(kn), q == 0 and part == 0, q == 2 and part == 2,
                                                   S["mm"] if part == 2 else None)

                @block.scalar
                def _(act):
                    chain = Chain(act, S["act_chain"])

                    def split_hi(c):
                        if c >= N_CHUNKS:
                            return
                        if c < 2:
                            act.wait_ge(prefetched, 32 * (l + 1))
                        else:
                            act.wait_ge(S[f"w_in{c % 2}"], 16 * loads(c))
                            act.wait_ge(S["mm"], mm_count(c - 2))
                        kt, w = chunk_shape(c)
                        nc.scalar.activation(whi[:, c % 2, 0:kt * w], raw[:, c % 2, 0:kt * w], ACT.Copy).then_inc(S["w_hi"], 1)

                    def norm_hi(tag, gain):
                        for k in range(KD):
                            act.wait_ge(S["hps" + tag], k + 1)
                            nc.scalar.activation(hhi[:, k, :], ps[:, k, :], ACT.Copy, scale=gain[:, k:k + 1]
                                                 ).then_inc(S["hhi" + tag], 1)

                    def ev(dst, src):
                        return nc.scalar.activation(dst, src, ACT.Copy)

                    def empty_group(n):
                        c, g, _ = GROUPS[n]
                        name = CHUNKS[c][0]
                        act.wait_ge(S["mm"], n + 1)
                        b = ps[:, n % IN_BANKS, :]
                        if name == "cmp":
                            if g == 0:
                                act.wait_ge(S["vbs"], 1)
                                act.wait_ge(S["gback"], 4)
                            for gg in range(2):
                                rows = slice(gg * HEAD, (gg + 1) * HEAD)
                                ev(x2[0:HEAD, g, gg, :], b[rows, :])
                                i = ev(x2[HEAD:P, g, gg, 0:T - 1], b[rows, 1:T])
                        elif name in ("gq", "gk", "gv"):
                            j = n
                            if j >= 2:
                                act.wait_ge(S["conv"], j - 1)
                            i = ev(gpre[:, j % 2, 0:T], b[:, :])
                        elif name == "zg":
                            ev(z[:, g, :], b[:, 0:GW])
                            i = ev(gbuf[:, g, :], b[:, GW:GW + 2 * GH])
                        elif name == "kvs":
                            i = ev(kv[:, g, 0:256], b[:, 0:256])
                        elif name == "kvw":
                            ev(kv[:, g, 256:512], b[:, 0:256])
                            i = ev(ngt[:, g, :], b[:, 256:256 + 3 * NH])
                        elif name == "cc":
                            act.wait_ge(S["conv"], 6)
                            i = ev(ccb[:, g, :], b[:, :])
                        else:
                            if name == "nq0" and g == 0:
                                act.wait_ge(S["cmp"], 1)
                            q0 = 0 if name == "nq0" else 256
                            i = ev(nq[:, g, q0:q0 + 256], b[:, 0:256])
                        i.then_inc(S["ev_act"], 1)

                    def hop_act(s):
                        t, i = divmod(s, 7)
                        if i not in (0, 1, 5, 6):
                            return
                        act.wait_ge(S["hop"], s + 1)
                        dst, bank = {0: (cM, 5), 1: (cM2, 6), 5: (cM4T, 7), 6: (vb[:, t, :], 3)}[i]
                        if i == 6:
                            ev(dst, ps[:, bank, 0:GW]).then_inc(S["hop_act"], 1)
                        else:
                            ev(dst, ps[:, bank, :].rearrange("p (h c) -> p h c", h=GH)).then_inc(S["hop_act"], 1)

                    split_hi(0)
                    act.wait_ge(S["norm_gains"], 32)
                    norm_hi("0", an)
                    split_hi(1)
                    slots = 0
                    for n in range(len(GROUPS)):
                        c, g, e = GROUPS[n]
                        last = n + 1 == len(GROUPS) or GROUPS[n + 1][0] != c
                        if n >= HOP_GROUP:
                            for _ in range(2):
                                if slots < 7 * NT:
                                    hop_act(slots)
                                    slots += 1
                        if last:
                            split_hi(c + 2)
                        if e == "act":
                            empty_group(n)
                        if n >= HOP_GROUP and slots < 7 * NT:
                            hop_act(slots)
                            slots += 1
                        if n == 20:
                            act.wait_ge(S["cmp_u"], 1)
                            nc.scalar.activation(hid[:, 2, :], hid[:, 1, :], ACT.Tanh, scale=0.7978845608028654
                                                 ).then_inc(S["cmp_th"], 1)
                        if n <= 5:
                            j = n
                            act.wait_ge(S["cy"], j + 1)
                            nc.scalar.activation(gpre[:, j % 2, 0:T], gcm[:, j % 2, :], ACT.Tanh).then_inc(S["th"], 1)
                        if 2 <= n <= 7:
                            j = n - 2
                            act.wait_ge(S["gtr"], j + 1)
                            ev(gtm[:, :, j * P:(j + 1) * P], ps[:, 3 + j % 3, :].rearrange("p (t c) -> p t c", t=NT)
                               ).then_inc(S["gtm"], 1)
                        if n == 6:
                            act.wait_ge(S["gtm"], 4)
                            nc.scalar.activation(L.rearrange("p (t a) b -> p t (a b)", t=NT), gtm[:, :, 0:2 * GW],
                                                 ACT.Square).then_inc(S["gsq"], 1)
                        if n == 9:
                            act.wait_ge(S["gy"], 1)
                            nc.scalar.activation(gsc[:, 1, :].rearrange("p (t h) -> p t h", t=NT), gbuf[:, :, 0:GH],
                                                 ACT.Tanh, scale=0.5)
                            nc.scalar.activation(alog[:], alog[:], ACT.Exp)
                            nc.scalar.activation(gsc[:, 8, :], gsc[:, 8, :], ACT.Exp, scale=-1.0).then_inc(S["gexp"], 1)
                            act.wait_ge(S["gexp1"], 1)
                            nc.scalar.activation(gsc[:, 8, :], gsc[:, 8, :], ACT.Ln).then_inc(S["gln"], 1)
                        if n == 10:
                            act.wait_ge(S["gcum"], 1)
                            nc.scalar.activation(gsc[:, 3, :], gsc[:, 2, :], ACT.Exp)
                            nc.scalar.activation(gsc[:, 5, :], gsc[:, 5, :], ACT.Exp)
                            nc.scalar.activation(gsc[:, 6, :], gsc[:, 7, :], ACT.Exp).then_inc(S["geg"], 1)
                            for i in range(4):
                                act.wait_ge(S["gback"], i + 1)
                                ev((qT, qT, kT, kT)[i][:, i % 2, :], ps[:, 3 + i, :]).then_inc(S["gT"], 1)
                        if n == 12:
                            for i in range(2):
                                act.wait_ge(S["gback"], 5 + i)
                                ev(qdT[:, i, :], ps[:, 7 if i == 0 else 3, :]).then_inc(S["gT"], 1)
                        if 13 <= n <= 16:
                            t = n - 13
                            act.wait_ge(S["dec"], t + 1)
                            nc.scalar.activation(dA, dA, ACT.Exp, scale=-1.0)
                            nc.scalar.activation(dB, dB, ACT.Exp).then_inc(S["dexp"], 1)
                        if n == 23:
                            act.wait_ge(S["d_out"], 32)
                            nc.scalar.activation(ngt[:], ngt[:], ACT.Tanh, scale=0.5).then_inc(S["ngth"], 1)
                            for br in range(2):
                                nc.scalar.activation(jq[:, br, :].rearrange("p (t c) -> p t c", t=NT),
                                                     kv[:, :, br * 256:br * 256 + P], ACT.Square).then_inc(S["ksq"], 1)
                        if 26 <= n <= 29:
                            t = n - 26
                            act.wait_ge(S["kred"], 2)
                            act.wait_ge(S["ev_act"], n + 1)
                            if t >= 2:
                                act.wait_ge(S["qred"], t - 1)
                            nc.scalar.activation(jq[:, t % 2, :], nq[:, t, :], ACT.Square).then_inc(S["qsq"], 1)

                    act.wait_ge(S["ev_dve"], 4)
                    for j in range(4):
                        act.wait_ge(S["qnps"], j + 1)
                        ev(qnT[:, j, :], ps[:, j, :]).then_inc(S["qnT"], 1)
                    for i in range(4):
                        br, g = divmod(i, 2)
                        act.wait_ge(S["kps"], br + 1)
                        for r in range(2):
                            ins = ev(kst[r * HEAD:(r + 1) * HEAD, i, :], ps[g * HEAD:(g + 1) * HEAD, 4 + br, :])
                        ins.then_inc(S["khi"], 1)
                    for h in range(NH):
                        act.wait_ge(S["qps"], h // 2 + 1)
                        rows = slice(h % 2 * HEAD, (h % 2 + 1) * HEAD)
                        ev(qst[rows, h, :], ps[rows, Q_BANKS[h // 2], :]).then_inc(S["qhi"], 1)

                    def exp(s):
                        i = s % NT
                        act.wait_ge(S["nmax"], s + 1)
                        if s >= 5:
                            act.wait_ge(S["ptr"], s - 4)
                        n = (i + 1) * P
                        nc.scalar.activation(prob[s % 5][:, 0:n], ps[:, i, 0:n], ACT.Exp, bias=att[:, 0, s % 8:s % 8 + 1],
                                             accum_out=att[:, 1, s % 8:s % 8 + 1]).then_inc(S["exp"], 1)

                    def evacuate(s):
                        act.wait_ge(S["ptr"], s + 1)
                        if s >= 3:
                            act.wait_ge(S["pv"], s - 2)
                        n = (s % NT + 1) * P
                        ev(pT[s % 3][:, 0:n], ps[:, 4 + s % 2, 0:n]).then_inc(S["pTe"], 1)

                    def mix_hi(m):
                        act.wait_ge(S["pv"], 16 * (m + 1))
                        ev(ahi[:, 2 + m, :], ps[:, 6, :]).then_inc(S["mix_hi"], 1)

                    for tick in range(N_ITEMS + LAG_EVACUATE):
                        if tick < N_ITEMS:
                            exp(tick)
                        s = tick - LAG_EVACUATE
                        if s >= 0:
                            evacuate(s)
                            if s % 16 == 0 and s > 0:
                                mix_hi(s // 16 - 1)
                        if tick == 4:
                            act.wait_ge(S["cmax"], 1)
                            nc.scalar.activation(Pc, Pc, ACT.Exp).then_inc(S["cexp"], 1)
                        if tick in CMP_TICKS:
                            par = CMP_TICKS.index(tick)
                            act.wait_ge(S["cpt"], par + 1)
                            ev(PcT[:, par, :], ps[:, 7, :]).then_inc(S["PcT"], 1)
                        if tick == OG_TICK:
                            act.wait_ge(S["oall"], 1)
                            nc.scalar.activation(zt, og, ACT.Square).then_inc(S["osq"], 1)
                        if tick == OG_TICK + 2:
                            act.wait_ge(S["ored"], 1)
                            nc.scalar.activation(zt, z, ACT.Tanh, scale=0.5).then_inc(S["zth"], 1)
                        if tick in (OG_TICK + 4, OG_TICK + 5):
                            m = tick - OG_TICK - 4
                            ev(ahi[:, 6 + m, :], ccb[:, m, :]).then_inc(S["mixc_hi"], 1)
                        if tick in (OG_TICK + 15, OG_TICK + 18):
                            m = (tick - OG_TICK - 15) // 3
                            act.wait_ge(S["ogT"], m + 1)
                            ev(ahi[:, m, :], ps[:, 7, :]).then_inc(S["mixg_hi"], 1)
                    mix_hi(NH // 2 - 1)

                    for c in range(N_IN, FFN0 - 1):
                        split_hi(c + 2)
                    for t in range(NT):
                        act.wait_ge(S["x_res"], 12 + t + 1)
                        norm_square(act, t, S["ssq1"])
                    norm_hi("1", fn)
                    split_hi(FFN0 + 1)
                    for f in range(2):
                        for i in range(FT):
                            c, cnt = FFN0 + f * PER_HALF + i, f * FT + i
                            split_hi(c + 2)
                            act.wait_ge(S["mm"], mm_count(c) - 1)
                            if cnt >= 2:
                                act.wait_ge(S["up_mul"], cnt - 1)
                            nc.scalar.activation(ft[:, cnt % 2, :], ps[:, 2 * (i % 2), :], ACT.Silu).then_inc(S["silu"], 1)
                            act.wait_ge(S["up_mul"], cnt + 1)
                            ev(ahi[:, i, :], ft[:, 2 + cnt % 2, :]).then_inc(S["a_hi"], 1)
                        for i in range(FT, PER_HALF):
                            split_hi(FFN0 + f * PER_HALF + i + 2)
                    for t in range(NT):
                        act.wait_ge(S["x_down"], 12 + t + 1)
                        norm_square(act, t, S["ssq_next"])

                @block.gpsimd
                def _(pool):
                    chain = Chain(pool, S["pool_chain"])

                    def split_lo(c):
                        if c >= N_CHUNKS:
                            return
                        pool.wait_ge(S["w_hi"], c + 1)
                        kt, w = chunk_shape(c)
                        nc.gpsimd.tensor_tensor(wlo[:, c % 2, 0:kt * w], raw[:, c % 2, 0:kt * w],
                                                whi[:, c % 2, 0:kt * w].bitcast(F32), ALU.subtract).then_inc(S["w_lo"], 1)

                    def scaled(dst, src, row):
                        s = gsc[:, row, :].rearrange("p (t h o) -> p t h o", t=NT, o=1).broadcast_to([P, NT, GH, HEAD])
                        return nc.gpsimd.tensor_tensor(dst.rearrange("p t (h d) -> p t h d", h=GH),
                                                       src.rearrange("p t (h d) -> p t h d", h=GH), s, ALU.mult)

                    def make_trig(t):
                        if t >= 2:
                            pool.wait_ge(S["gr"], t - 1)
                        for h in range(GH):
                            ins = nc.gpsimd.tensor_scalar(trig[:, t % 2, h * P:(h + 1) * P], tri[:],
                                                          gsc[:, 0, t * GH + h:t * GH + h + 1], None, ALU.mult)
                        ins.then_inc(S["trig"], 1)

                    def one_minus(t):
                        pool.wait_ge(S["hop"], 7 * t + 2)
                        pool.wait_ge(S["hop_dve"], 6 * t + 1)
                        idb = ident[:].rearrange("p (o c) -> p o c", o=1).broadcast_to([P, GH, P])
                        nc.gpsimd.tensor_tensor(cMT, idb, cMT, ALU.subtract).then_inc(S["hop_pool"], 1)

                    def newton(y, v, w):
                        for _ in range(3):
                            chain(nc.gpsimd.tensor_tensor(w, y, y, ALU.mult))
                            chain(nc.gpsimd.tensor_tensor(w, w, v, ALU.mult))
                            chain(nc.gpsimd.tensor_scalar(w, w, -0.5, 1.5, ALU.mult, ALU.add))
                            chain(nc.gpsimd.tensor_tensor(y, w, y, ALU.mult))

                    nc.gpsimd.memset(state[:], 0.0).then_inc(S["szero"], 1)
                    split_lo(0)
                    split_lo(1)
                    pool.wait_ge(S["hps0"], KD)
                    chain(nc.gpsimd.memset(Ti, 0.0))
                    nc.gpsimd.affine_select(out=Ti, in_=Ti, compare_op=ALU.not_equal, fill=1.0, base=0,
                                            pattern=[[-1, 16], [1, 16]], channel_multiplier=0).then_inc(S["tiinit"], 1)
                    split_lo(2)
                    split_lo(3)
                    split_lo(4)
                    pool.wait_ge(S["g"], 1)
                    make_trig(0)
                    make_trig(1)
                    pool.wait_ge(S["geg2"], 1)
                    pool.wait_ge(S["gtm"], 6)
                    pool.wait_ge(S["qkn"], 1)
                    scaled(qd, gtm[:, :, 0:GW], 3).then_inc(S["qdec"], 1)
                    split_lo(5)
                    scaled(kbe, gtm[:, :, GW:2 * GW], 4)
                    scaled(kdec, gtm[:, :, GW:2 * GW], 5)
                    scaled(vb, gtm[:, :, 2 * GW:3 * GW], 1).then_inc(S["vbs"], 1)
                    make_trig(2)
                    make_trig(3)
                    split_lo(6)
                    pool.wait_ge(S["gr"], NT)
                    nc.gpsimd.memset(at(11264, 4096), 0.0).then_inc(S["tdzero"], 1)
                    split_lo(7)
                    pool.wait_ge(S["d_in"], 128)
                    ob = offblk[:].rearrange("p (o c) -> p o c", o=1).broadcast_to([P, NT * GH, P])
                    nc.gpsimd.tensor_tensor(L, L, ob, ALU.mult).then_inc(S["Lmask"], 1)
                    split_lo(8)
                    split_lo(9)
                    one_minus(0)
                    split_lo(10)
                    one_minus(1)
                    split_lo(11)
                    one_minus(2)
                    pool.wait_ge(S["qseed"], 1)
                    newton(st[:, 4, :], st[:, 2, :], st[:, 6, :])
                    nc.gpsimd.tensor_scalar(st[:, 4, :], st[:, 4, :], HEAD ** -0.5, None, ALU.mult
                                            ).then_inc(S["qrms"], 1)
                    one_minus(3)
                    split_lo(12)
                    pool.wait_ge(S["roped"], 1)
                    nc.gpsimd.memset(Pc, 2 * NEG).then_inc(S["cmem"], 1)
                    pc = Pc.rearrange("p a b c -> p (a b) c")
                    per_row = lambda r: r.rearrange("p (n o) -> p n o", o=1).broadcast_to([P, 32, 32])
                    pool.wait_ge(S["cmx"], 1)
                    nc.gpsimd.tensor_tensor(pc, pc, per_row(st[:, 0, :]), ALU.subtract).then_inc(S["cmax"], 1)
                    split_lo(13)
                    pool.wait_ge(S["cfac"], 1)
                    chain(nc.gpsimd.tensor_tensor(pc, pc, per_row(st[:, 1, :]), ALU.mult))
                    for par in range(2):
                        v = Pc[:, par].rearrange("p (t j) c -> p t j c", j=4)
                        ins = nc.gpsimd.tensor_tensor(v, v, cok[:].rearrange("p t (o c) -> p t o c", o=1)
                                                      .broadcast_to([P, NT, 4, 32]), ALU.mult)
                    ins.then_inc(S["cprob"], 1)
                    o3 = og.rearrange("p t (h d) -> p (t h) d", d=HEAD)
                    pool.wait_ge(S["oseed"], 1)
                    newton(st[:, 2, 0:16], st[:, 1, 0:16], st[:, 3, 0:16])
                    chain(nc.gpsimd.tensor_tensor(o3, o3, st[:, 2, 0:16].rearrange("p (n o) -> p n o", o=1)
                                                  .broadcast_to([P, 16, HEAD]), ALU.mult))
                    chain(nc.gpsimd.tensor_tensor(o3, o3, gng[:].rearrange("p (o d) -> p o d", o=1).broadcast_to([P, 16, HEAD]), ALU.mult))
                    pool.wait_ge(S["zth"], 1)
                    chain(nc.gpsimd.tensor_scalar(zt, zt, 0.5, 0.5, ALU.mult, ALU.add))
                    chain(nc.gpsimd.tensor_tensor(zt, zt, z, ALU.mult))
                    nc.gpsimd.tensor_tensor(og, og, zt, ALU.mult).then_inc(S["og"], 1)
                    for c in range(14, N_CHUNKS):
                        split_lo(c)

                @block.vector
                def _(dve):
                    chain = Chain(dve, S["dve_chain"])
                    V = nc.vector

                    def norm_lo(tag, gain):
                        for k in range(KD):
                            dve.wait_ge(S["hhi" + tag], k + 1)
                            V.scalar_tensor_tensor(out=hlo[:, k, :], in0=ps[:, k, :], scalar=gain[:, k:k + 1],
                                                   in1=hhi[:, k, :].bitcast(F32), op0=ALU.mult, op1=ALU.subtract
                                                   ).then_inc(S["hlo" + tag], 1)

                    def conv(j):
                        dve.wait_ge(S["ev_act"], j + 1)
                        if j >= 2:
                            dve.wait_ge(S["gtr"], j - 1)
                        y, v = gcm[:, j % 2, :], gpre[:, j % 2, :]
                        chain(V.tensor_scalar(y, v[:, 0:T], cw[:, j, 3:4], None, ALU.mult))
                        for d in range(1, 4):
                            ins = V.scalar_tensor_tensor(out=y[:, d:T], in0=v[:, 0:T - d], scalar=cw[:, j, 3 - d:4 - d],
                                                         in1=y[:, d:T], op0=ALU.mult, op1=ALU.add)
                            if d < 3:
                                chain(ins)
                        ins.then_inc(S["cy"], 1)
                        dve.wait_ge(S["th"], j + 1)
                        V.scalar_tensor_tensor(out=y, in0=v[:, 0:T], scalar=1.0, in1=y, op0=ALU.add, op1=ALU.mult
                                               ).then_inc(S["conv"], 1)

                    def cmp_hidden():
                        dve.wait_ge(S["cmp"], 1)
                        for k in range(2):
                            chain(V.tensor_copy(peb[:, k:k + 1], ps[0:HEAD, 3, k * P + 2 * NC:k * P + 2 * NC + 1]))
                        for k in range(2):
                            cols = slice(k * 2 * NC, (k + 1) * 2 * NC)
                            chain(V.tensor_scalar(hid[:, 0, cols], ps[0:HEAD, 3, k * P:k * P + 2 * NC], peb[:, k:k + 1], None, ALU.add))
                        chain(V.tensor_tensor(hid[:, 1, :], hid[:, 0, :], hid[:, 0, :], ALU.mult))
                        chain(V.tensor_scalar(hid[:, 1, :], hid[:, 1, :], 0.044715, 1.0, ALU.mult, ALU.add))
                        V.tensor_tensor(hid[:, 1, :], hid[:, 1, :], hid[:, 0, :], ALU.mult).then_inc(S["cmp_u"], 1)
                        dve.wait_ge(S["cmp_th"], 1)
                        chain(V.scalar_tensor_tensor(out=hid[:, 1, :], in0=hid[:, 2, :], scalar=1.0, in1=hid[:, 0, :],
                                                     op0=ALU.add, op1=ALU.mult))
                        V.tensor_scalar(hid[:, 0, :], hid[:, 1, :], 0.5, None, ALU.mult).then_inc(S["cmp_hid"], 1)

                    def cmp_norm():
                        dve.wait_ge(S["cmp"], 2)
                        chain(V.tensor_copy(kcn[0:NC, 0, :], ps[0:NC, 7, 0:P]))
                        for j in range(4):
                            chain(V.tensor_copy(vcr[32 * j:32 * j + NC, :], ps[0:NC, 7, P + (j // 2) * HEAD:P + (j // 2 + 1) * HEAD]))
                        chain(V.tensor_tensor(kcn[0:NC, 1, :], kcn[0:NC, 0, :], kcn[0:NC, 0, :], ALU.mult))
                        chain(V.tensor_reduce(st[0:NC, 4, 0:2], kcn[0:NC, 1, :].rearrange("p (g d) -> p g d", g=2), AX, ALU.add))
                        chain(V.tensor_scalar(st[0:NC, 5, 0:2], st[0:NC, 4, 0:2], 1.0 / HEAD, EPS, ALU.mult, ALU.add))
                        rsqrt(chain, st[0:NC, 6, 0:2], st[0:NC, 5, 0:2], st[0:NC, 7, 0:2])
                        for g in range(NG):
                            ins = V.scalar_tensor_tensor(out=kcn[0:NC, 0, g * HEAD:(g + 1) * HEAD], in0=kcn[0:NC, 0, g * HEAD:(g + 1) * HEAD],
                                                         scalar=st[0:NC, 6, g:g + 1], in1=kg[0:NC, 0, :], op0=ALU.mult, op1=ALU.mult)
                        ins.then_inc(S["cmp_kn"], 1)

                    def cmp_keys():
                        dve.wait_ge(S["cmp"], 3)
                        for g in range(NG):
                            for r in range(2):
                                ins = V.tensor_copy(kcT[r * HEAD:(r + 1) * HEAD, g, r, 0:NC], ps[g * HEAD:(g + 1) * HEAD, 7, 0:NC])
                        ins.then_inc(S["kcT"], 1)

                    def l2_norms():
                        dve.wait_ge(S["gsq"], 1)
                        chain(V.tensor_reduce(st[:, 0, :], L.rearrange("p a (b d) -> p (a b) d", d=HEAD), AX, ALU.add))
                        chain(V.tensor_scalar(st[:, 1, :], st[:, 0, :], EPS, None, ALU.add))
                        rsqrt(chain, st[:, 2, :], st[:, 1, :], st[:, 3, :])
                        q_r = st[:, 2, :].rearrange("p (t a) -> p t a", t=NT)[:, :, 0:GH]
                        chain(V.tensor_scalar(q_r, q_r, HEAD ** -0.5, None, ALU.mult))
                        r4 = st[:, 2, :].rearrange("p (t a o) -> p t a o", t=NT, o=1).broadcast_to([P, NT, 2 * GH, HEAD])
                        v = gtm[:, :, 0:2 * GW].rearrange("p t (a d) -> p t a d", d=HEAD)
                        V.tensor_tensor(v, v, r4, ALU.mult).then_inc(S["qkn"], 1)

                    def gates():
                        y, a = gsc[:, 7, :], gsc[:, 8, :]
                        th4 = lambda r: r.rearrange("p (t h) -> p t h", t=NT)
                        row4 = lambda v: v[:].rearrange("p (o h) -> p o h", o=1).broadcast_to([P, NT, GH])
                        dve.wait_ge(S["ev_act"], 10)
                        chain(V.tensor_tensor(th4(y), gbuf[:, :, GH:2 * GH], row4(dtb), ALU.add))
                        V.scalar_tensor_tensor(out=a, in0=y, scalar=-1.0, in1=y, op0=ALU.mult, op1=ALU.max).then_inc(S["gy"], 1)
                        dve.wait_ge(S["gexp"], 1)
                        chain(V.tensor_scalar(gsc[:, 1, :], gsc[:, 1, :], 0.5, 0.5, ALU.mult, ALU.add))
                        V.tensor_scalar(a, a, 1.0, None, ALU.add).then_inc(S["gexp1"], 1)
                        dve.wait_ge(S["gln"], 1)
                        chain(V.scalar_tensor_tensor(out=a, in0=y, scalar=0.0, in1=a, op0=ALU.max, op1=ALU.add))
                        V.scalar_tensor_tensor(out=th4(gsc[:, 0, :]), in0=th4(a), scalar=-1.0, in1=row4(alog), op0=ALU.mult,
                                               op1=ALU.mult).then_inc(S["g"], 1)

                    def gate_sums():
                        dve.wait_ge(S["gsum"], 1)
                        chain(V.tensor_copy(gsc[:, 2, :], ps[:, 7, 0:16]))
                        chain(V.tensor_copy(gsc[:, 7, :], ps[:, 7, 16:32]))
                        V.tensor_tensor(gsc[:, 5, :], gsc[:, 7, :], gsc[:, 2, :], ALU.subtract).then_inc(S["gcum"], 1)
                        dve.wait_ge(S["geg"], 1)
                        V.tensor_tensor(gsc[:, 4, :], gsc[:, 1, :], gsc[:, 3, :], ALU.mult).then_inc(S["geg2"], 1)
                        for par in range(2):
                            rows = slice(par * HEAD, (par + 1) * HEAD)
                            ins = V.tensor_copy(glc[rows], gsc[rows, 6, :].rearrange("p (t j r) -> p t j r", t=NT, r=2)[:, :, :, par])
                        ins.then_inc(S["scan"], 1)

                    def decays(t):
                        dve.wait_ge(S["gr"], t + 1)
                        if t:
                            dve.wait_ge(S["A"], t)
                        for h in range(GH):
                            g0 = gsc[:, 2, t * GH + h:t * GH + h + 1]
                            V.tensor_scalar(dA[:, h, :], ps[:, 7, h * P:(h + 1) * P], g0, 0.0, ALU.subtract, ALU.max)
                            ins = V.tensor_scalar(dB[:, h, :], ps[:, 7, h * P:(h + 1) * P], g0, 0.0, ALU.subtract, ALU.min)
                        ins.then_inc(S["dec"], 1)
                        dve.wait_ge(S["dexp"], t + 1)
                        for h in range(GH):
                            ins = V.scalar_tensor_tensor(out=dA[:, h, :], in0=dA[:, h, :], scalar=gsc[:, 1, t * GH + h:t * GH + h + 1],
                                                         in1=below[:], op0=ALU.mult, op1=ALU.mult)
                        chain(V.tensor_tensor(dB, dB, tri[:].rearrange("p (o c) -> p o c", o=1).broadcast_to([P, GH, P]), ALU.mult))
                        dve.wait_ge(S["gram"], t + 1)
                        for par in range(2):
                            q0 = t * GH + par
                            for bank, dec, dst in ((3 + par, dA, L), (5 + par, dB, qkT)):
                                ins = V.tensor_tensor(dst[:, q0:q0 + 3:2, :], ps[:, bank, 0:256].rearrange("p (j c) -> p j c", j=2),
                                                      dec[:, par:par + 3:2, :], ALU.mult)
                        ins.then_inc(S["A"], 1)

                    def diag_solve():
                        dve.wait_ge(S["Dm"], 16)
                        dve.wait_ge(S["tiinit"], 1)
                        for i in range(1, 16):
                            a = Ti[:, 0:i, 0:i].rearrange("p j m -> p m j")
                            d = Dm[:, i:i + 1, 0:i].broadcast_to([P, i, i])
                            tmp = dtmp[:, 0:i, 0:i]
                            chain(V.tensor_tensor(tmp, a, d, ALU.mult))
                            chain(V.tensor_reduce(Ti[:, i, 0:i], tmp, AX, ALU.add, negate=True))
                        V.tensor_copy(Tt, Ti.rearrange("p i j -> p j i")).then_inc(S["Tt"], 1)

                    def short_conv(m):
                        v, y = cpre[:, m, 0:T], ccb[:, m, :]
                        chain(V.tensor_scalar(y, v, scw[:, m, 2:3], None, ALU.mult))
                        for d in range(1, 3):
                            chain(V.scalar_tensor_tensor(out=y[:, d:T], in0=v[:, 0:T - d], scalar=scw[:, m, 2 - d:3 - d],
                                                         in1=y[:, d:T], op0=ALU.mult, op1=ALU.add))

                    def k4(br):
                        return kv[:, :, br * 256:br * 256 + P].rearrange("p t (g d) -> p t g d", g=NG)

                    def k_norm(br):
                        k, r3 = k4(br), st[:, 5, br * 8:(br + 1) * 8].rearrange("p (t g o) -> p t g o", t=NT, o=1)
                        chain(V.tensor_tensor(k, k, r3.broadcast_to([P, NT, NG, HEAD]), ALU.mult))
                        chain(V.tensor_tensor(k, k, kg[:, 1 + br:2 + br, :].rearrange("p (o a) d -> p o a d", o=1)
                                              .broadcast_to([P, NT, NG, HEAD]), ALU.mult))

                    def rope(v, n):
                        cs, sn = (cossin[:, i].rearrange("p t (o f) -> p t o f", o=1).broadcast_to([P, NT, n, HALF]) for i in range(2))
                        x1c, x2s, x1s = (rot[:, i, 0:NT * n * HALF].rearrange("p (t h f) -> p t h f", t=NT, f=HALF) for i in range(3))
                        if n == NG:
                            x1c, x2s, x1s = (ktmp[:, i].rearrange("p (t h f) -> p t h f", t=NT, f=HALF) for i in range(3))
                        lo_, hi_ = v[:, :, :, 0:HALF], v[:, :, :, HALF:ROT]
                        V.tensor_tensor(x1c, lo_, cs, ALU.mult)
                        V.tensor_tensor(x2s, hi_, sn, ALU.mult)
                        chain(V.tensor_tensor(x1s, lo_, sn, ALU.mult))
                        chain(V.tensor_tensor(lo_, x1c, x2s, ALU.subtract))
                        chain(V.tensor_tensor(x1c, hi_, cs, ALU.mult))
                        chain(V.tensor_tensor(hi_, x1c, x1s, ALU.add))

                    def q_statistics():
                        dve.wait_ge(S["qred"], NT)
                        chain(V.tensor_scalar(st[:, 2, :], st[:, 0, :], 1.0 / HEAD, EPS, ALU.mult, ALU.add))
                        V.tensor_scalar(st[:, 4, :].bitcast(I32), st[:, 2, :].bitcast(I32), -0.5, RSQRT_SEED,
                                        ALU.mult, ALU.add).then_inc(S["qseed"], 1)

                    def q_norm(t):
                        if t == 0:
                            dve.wait_ge(S["qrms"], 1)
                        q3 = nq[:, t, :].rearrange("p (h d) -> p h d", h=NH)
                        r3 = st[:, 4, t * 8:(t + 1) * 8].rearrange("p (h o) -> p h o", o=1)
                        chain(V.tensor_tensor(q3, q3, r3.broadcast_to([P, NH, HEAD]), ALU.mult))
                        ins = V.tensor_tensor(q3, q3, qg[:].rearrange("p (o d) -> p o d", o=1).broadcast_to([P, NH, HEAD]), ALU.mult)
                        if t == NT - 1:
                            ins.then_inc(S["qn"], 1)

                    def hop_dve(s):
                        t, i = divmod(s, 7)
                        if i == 5:
                            return
                        dve.wait_ge(S["hop"], s + 1)
                        if i == 2 or i == 3:
                            pass
                        bank = {0: 4, 1: 7, 2: 4, 3: 5, 4: 6, 6: 4}[i]
                        src = ps[:, bank, :].rearrange("p (h c) -> p h c", h=GH)
                        if i == 0:
                            ins = V.tensor_copy(cMT, src)
                        elif i == 1:
                            ins = V.tensor_copy(cM2T, src)
                        elif i == 2:
                            ins = V.tensor_copy(cM4T, src)
                        elif i == 3:
                            ins = V.tensor_tensor(cZ1, src, TD[:, t * GH:(t + 1) * GH, :], ALU.add)
                        elif i == 4:
                            ins = V.tensor_tensor(cM, src, cZ1, ALU.add)
                        else:
                            ins = V.tensor_copy(wT[:, :, t * P:(t + 1) * P], ps[:, 4, 0:256].rearrange("p (j c) -> p j c", j=2))
                        ins.then_inc(S["hop_dve"], 1)

                    dve.wait_ge(S["norm_gains"], 32)
                    norm_lo("0", an)
                    dve.wait_ge(S["params"], 16 * N_PARAMS)
                    chain(V.tensor_scalar(cw[:], cw[:], 0.5, None, ALU.mult))
                    slots = 0
                    for n in range(len(GROUPS)):
                        name, g = CHUNKS[GROUPS[n][0]][0], GROUPS[n][1]
                        if n >= HOP_GROUP:
                            for _ in range(2):
                                if slots < 7 * NT:
                                    hop_dve(slots)
                                    slots += 1
                        if n == 20:
                            cmp_hidden()
                        if n == 21:
                            cmp_norm()
                        if n == 23:
                            cmp_keys()
                        if n <= 5:
                            conv(n)
                        if n == 6:
                            l2_norms()
                        if n == 9:
                            gates()
                        if n == 10:
                            gate_sums()
                        if 13 <= n <= 16:
                            decays(n - 13)
                        if n == 17:
                            diag_solve()
                        if n == 23:
                            dve.wait_ge(S["ngth"], 1)
                            chain(V.tensor_scalar(ngt[:], ngt[:], 0.5, 0.5, ALU.mult, ALU.add))
                            for br in range(2):
                                dve.wait_ge(S["ksq"], br + 1)
                                V.tensor_reduce(st[:, 1, br * 8:(br + 1) * 8], jq[:, br, :].rearrange("p (a d) -> p a d", d=HEAD),
                                                AX, ALU.add).then_inc(S["kred"], 1)
                            dve.wait_ge(S["kred"], 2)
                            chain(V.tensor_scalar(st[:, 3, 0:16], st[:, 1, 0:16], 1.0 / HEAD, EPS, ALU.mult, ALU.add))
                            rsqrt(chain, st[:, 5, 0:16], st[:, 3, 0:16], st[:, 7, 0:16])
                        if n in (24, 25):
                            k_norm(n - 24)
                        if n in (26, 27):
                            rope(k4(n - 26), NG)
                            if n == 27:
                                dve.nop().then_inc(S["kn"], 1)
                        if 27 <= n <= 30:
                            t = n - 27
                            dve.wait_ge(S["qsq"], t + 1)
                            V.tensor_reduce(st[:, 0, t * 8:(t + 1) * 8], jq[:, t % 2, :].rearrange("p (a d) -> p a d", d=HEAD),
                                            AX, ALU.add).then_inc(S["qred"], 1)
                        if n == 30:
                            q_statistics()
                        if 31 <= n <= 33:
                            q_norm(n - 31)
                            if n == 33:
                                q_norm(3)
                        if name == "cx":
                            dve.wait_ge(S["mm"], n + 1)
                            dve.wait_ge(S["ev_act"], emptied(n - 1)[1] if g == 0 else emptied(n - 2)[1])
                            dve.wait_ge(S["gtr"], 6)
                            V.tensor_tensor(cpre[:, g, 0:T], ps[:, n % IN_BANKS, :], ccb[:, g, :], ALU.mult).then_inc(S["ev_dve"], 1)
                        if name == "cb":
                            dve.wait_ge(S["mm"], n + 1)
                            V.tensor_tensor(ccb[:, g, :], ps[:, n % IN_BANKS, :], ccb[:, g, :], ALU.mult).then_inc(S["ev_dve"], 1)
                        if n >= HOP_GROUP and slots < 7 * NT:
                            hop_dve(slots)
                            slots += 1
                        if name == "cx":
                            dve.wait_ge(S["ev_dve"], g + 1)
                            short_conv(g)

                    dve.wait_ge(S["qnps"], 4)
                    rope(nq.rearrange("p t (h d) -> p t h d", h=NH), NH)
                    dve.nop().then_inc(S["roped"], 1)
                    for i in range(4):
                        br, g = divmod(i, 2)
                        dve.wait_ge(S["khi"], i + 1)
                        rows, other = slice(g * HEAD, (g + 1) * HEAD), slice((1 - g) * HEAD, (2 - g) * HEAD)
                        chain(V.tensor_tensor(kst[rows, 4 + i, :], ps[rows, 4 + br, :], kst[rows, i, :].bitcast(F32), ALU.subtract))
                        V.tensor_copy(kst[other, 4 + i, :], kst[rows, 4 + i, :].bitcast(F32)).then_inc(S["klo"], 1)
                    for h in range(NH):
                        dve.wait_ge(S["qhi"], h + 1)
                        rows, other = (slice((h + i) % 2 * HEAD, ((h + i) % 2 + 1) * HEAD) for i in range(2))
                        ins = V.tensor_tensor(qst[other, h, :], ps[rows, Q_BANKS[h // 2], :], qst[rows, h, :].bitcast(F32), ALU.subtract)
                        if h % 2:
                            ins.then_inc(S["qlo"], 1)

                    def cmp_softmax(step):
                        cst, cfac = st[:, 0, :], st[:, 1, :]
                        if step == 0:
                            dve.wait_ge(S["cmem"], 1)
                            for b in range(2):
                                dve.wait_ge(S["csc"], b + 1)
                                for par in range(2):
                                    V.tensor_tensor(Pc[:, par].rearrange("p (t j) c -> p j t c", j=4)[:, 2 * b:2 * b + 2, :, 0:NC],
                                                    ps[:, 2 + b, :].rearrange("p (j t r c) -> p r j t c", j=2, t=NT, r=2)[:, par, :, :, 0:NC],
                                                    cneg[:, :, 0:NC].rearrange("p (o t) c -> p o t c", o=1).broadcast_to([P, 2, NT, NC]),
                                                    ALU.add).then_inc(S["cadd"], 1)
                        elif step == 1:
                            dve.wait_ge(S["cadd"], 4)
                            V.tensor_reduce(cst, Pc.rearrange("p a b c -> p (a b) c")[:, :, 0:NC], AX, ALU.max).then_inc(S["cmx"], 1)
                        else:
                            dve.wait_ge(S["cexp"], 1)
                            chain(V.tensor_reduce(cst, Pc.rearrange("p a b c -> p (a b) c")[:, :, 0:NC], AX, ALU.add))
                            chain(V.reciprocal(cst, cst))
                            for par in range(2):
                                ins = V.tensor_tensor(cfac.rearrange("p (r t j) -> p r t j", r=2, j=4)[:, par],
                                                      cst.rearrange("p (r t j) -> p r t j", r=2, j=4)[:, par],
                                                      ngt[:].rearrange("p t (j r b) -> p r b t j", j=4, r=2)[:, par, 0], ALU.mult)
                            ins.then_inc(S["cfac"], 1)

                    def maximum(s):
                        i = s % NT
                        dve.wait_ge(S["score"], s + 1)
                        V.tensor_reduce(att[:, 0, s % 8:s % 8 + 1], ps[:, i, 0:(i + 1) * P], AX, ALU.max, negate=True
                                        ).then_inc(S["nmax"], 1)

                    def invert_sum(s):
                        dve.wait_ge(S["exp"], s + 1)
                        a = att[:, 1, s % 8:s % 8 + 1]
                        V.reciprocal(a, a).then_inc(S["inverse"], 1)

                    def scale_probs(s):
                        u, i = divmod(s, NT)
                        h, br = divmod(u, 2)
                        dve.wait_ge(S["inverse"], s + 1)
                        a = att[:, 1, s % 8:s % 8 + 1]
                        p_ap = prob[s % 5][:, 0:(i + 1) * P]
                        V.tensor_scalar(p_ap, p_ap, a, ngt[:, i, 3 * h + 1 + br:3 * h + 2 + br], ALU.mult, ALU.mult
                                        ).then_inc(S["pscaled"], 1)

                    def recurrence(t, part):
                        if part == 0:
                            dve.wait_ge(S["wS"], t + 1)
                            V.tensor_tensor(vnew, vb[:, t, :], ps[:, 7, 0:GW], ALU.subtract).then_inc(S["vnew"], 1)
                            return
                        dve.wait_ge(S["oS"], t + 1)
                        V.tensor_copy(og[:, t, :], ps[:, 7, 256:512])
                        for j in range(2):
                            for par in range(2):
                                r = slice(par * HEAD, (par + 1) * HEAD)
                                ins = V.scalar_tensor_tensor(out=state[r, j, r], in0=state[r, j, r], scalar=glc[r, t, j:j + 1],
                                                             in1=ps[r, 7, j * P + par * HEAD:j * P + (par + 1) * HEAD],
                                                             op0=ALU.mult, op1=ALU.add)
                        ins.then_inc(S["state"], 1)

                    def gdn_finish(part):
                        if part == 0:
                            dve.wait_ge(S["osq"], 1)
                            V.tensor_reduce(st[:, 0, 0:16], zt.rearrange("p t (h d) -> p (t h) d", d=HEAD), AX, ALU.add
                                            ).then_inc(S["ored"], 1)
                        else:
                            dve.wait_ge(S["ored"], 1)
                            chain(V.tensor_scalar(st[:, 1, 0:16], st[:, 0, 0:16], 1.0 / HEAD, EPS, ALU.mult, ALU.add))
                            V.tensor_scalar(st[:, 2, 0:16].bitcast(I32), st[:, 1, 0:16].bitcast(I32), -0.5, RSQRT_SEED,
                                            ALU.mult, ALU.add).then_inc(S["oseed"], 1)

                    def lo_part(dst, full, hi, done):
                        V.tensor_tensor(dst, full, hi.bitcast(F32), ALU.subtract).then_inc(done, 1)

                    cmp_softmax(0)
                    for tick in range(N_ITEMS + LAG_SCALE):
                        if tick < N_ITEMS:
                            maximum(tick)
                        if 0 <= tick - LAG_INVERT < N_ITEMS:
                            invert_sum(tick - LAG_INVERT)
                        s = tick - LAG_SCALE
                        if s >= 0:
                            scale_probs(s)
                        s = tick - LAG_EVACUATE
                        if s > 0 and s % 16 == 0 and s < N_ITEMS:
                            m = s // 16 - 1
                            dve.wait_ge(S["mix_hi"], m + 1)
                            lo_part(alo[:, MIX_LO[2 + m], :], ps[:, 6, :], ahi[:, 2 + m, :], S["mix_lo"])
                        if tick in (1, 5):
                            cmp_softmax(1 if tick == 1 else 2)
                        t, step = divmod(tick - RECUR_TICK, RECUR_PERIOD)
                        if 0 <= t < NT and step in (1, RECUR_SECOND + 1):
                            recurrence(t, int(step > 1))
                        if tick == OG_TICK - 1:
                            dve.wait_ge(S["state"], NT)
                            dve.nop().then_inc(S["oall"], 1)
                        if tick in (OG_TICK + 1, OG_TICK + 2):
                            gdn_finish(tick - OG_TICK - 1)
                        if tick in (OG_TICK + 7, OG_TICK + 8):
                            m = tick - OG_TICK - 7
                            dve.wait_ge(S["mixc_hi"], m + 1)
                            lo_part(alo[:, MIX_LO[6 + m], :], ccb[:, m, :], ahi[:, 6 + m, :], S["mixc_lo"])
                        if tick in (OG_TICK + 16, OG_TICK + 19):
                            m = (tick - OG_TICK - 16) // 3
                            dve.wait_ge(S["mixg_hi"], m + 1)
                            lo_part(alo[:, MIX_LO[m], :], ps[:, 7, :], ahi[:, m, :], S["mixg_lo"])
                    m = NH // 2 - 1
                    dve.wait_ge(S["mix_hi"], m + 1)
                    lo_part(alo[:, MIX_LO[2 + m], :], ps[:, 6, :], ahi[:, 2 + m, :], S["mix_lo"])

                    for c in range(N_OUT):
                        for t in range(NT):
                            dve.wait_ge(S["mm"], mm_count(N_IN + c - 1) + t + 1)
                            xs = x[:, t, c * 256:(c + 1) * 256]
                            V.tensor_tensor(xs, ps[:, 4 + t, 0:256], xs, ALU.add).then_inc(S["x_res"], 1)
                            if c == N_OUT - 1 and t:
                                norm_scale(dve, chain, (t - 1, t), S["ssq1"], S["hn1"])
                    norm_scale(dve, chain, (NT - 1, NT), S["ssq1"], S["hn1"])
                    norm_lo("1", fn)
                    for f in range(2):
                        for i in range(FT):
                            c, cnt = FFN0 + f * PER_HALF + i, f * FT + i
                            dve.wait_ge(S["silu"], cnt + 1)
                            dve.wait_ge(S["mm"], mm_count(c))
                            if cnt >= 2:
                                dve.wait_ge(S["a_lo"], cnt - 1)
                            V.tensor_tensor(ft[:, 2 + cnt % 2, :], ps[:, 2 * (i % 2) + 1, :], ft[:, cnt % 2, :], ALU.mult
                                            ).then_inc(S["up_mul"], 1)
                            dve.wait_ge(S["a_hi"], cnt + 1)
                            lo_part(alo[:, i, :], ft[:, 2 + cnt % 2, :], ahi[:, i, :], S["a_lo"])
                        for ch in range(2):
                            c = FFN0 + f * PER_HALF + FT + ch * 3 + 2
                            for t in range(NT):
                                dve.wait_ge(S["mm"], mm_count(c - 1) + t + 1)
                                xs = x[:, t, ch * 512:(ch + 1) * 512]
                                V.tensor_tensor(xs, ps[:, (4 if ch == 0 else 0) + t, :], xs, ALU.add).then_inc(S["x_down"], 1)
                                if f == 1 and ch == 1 and t:
                                    norm_scale(dve, chain, (t - 1, t), S["ssq_next"], S["hn_next"])
                    norm_scale(dve, chain, (NT - 1, NT), S["ssq_next"], S["hn_next"])
            clear()

        with nc.Block() as block:
            @block.sync
            def _(sp):
                sp.dma_start(out[0].rearrange("(t p) d -> p t d", p=P), x[:]).then_inc(S["stored"], 16)
                sp.wait_ge(S["stored"], 16)
                sp.wait_ge(prefetched, 32 * (DEPTH + 1))


_INS = ["x", "positions", "attn_norm", "w_in", "gdn_conv_w", "gdn_a_log", "gdn_dt_bias", "gdn_norm", "nsa_q_norm",
        "nsa_k_norm", "nsa_cmp_pe", "nsa_cmp_w1", "nsa_cmp_w2", "conv_w", "w_out", "ffn_norm", "w_gate_up", "w_down"]


def kernel(**inputs):
    import numpy as _np
    import concourse.bacc as _bacc
    from concourse import mybir as _mybir
    from concourse.bass_utils import run_bass_kernel_spmd as _run

    nc = _bacc.Bacc("TRN2", target_bir_lowering=False, num_devices=1)
    arrays, aps = {}, {}
    for name in _INS:
        a = _np.ascontiguousarray(inputs[name])
        arrays[f"in_{name}"] = a
        aps[name] = nc.dram_tensor(f"in_{name}", a.shape, _mybir.dt.from_np(a.dtype), kind="ExternalInput").ap()
    out = nc.dram_tensor("out", inputs["x"].shape, F32, kind="ExternalOutput").ap()
    trunk(nc, aps, out)
    r = _run(nc, [arrays], core_ids=[0])
    return r.results[0]["out"]
```
